# Optimizing a Trainium2 kernel written in Bass

```python
import jax, jax.numpy as jnp
from jax import lax
import numpy as np

D_MODEL = 1024
BATCH = 1
SEQ = 256
DEPTH = 2

MLA_HEADS = 16
MLA_Q_RANK = 384
MLA_KV_RANK = 256
MLA_NOPE = 64
MLA_ROPE = 32
MLA_QK = MLA_NOPE + MLA_ROPE
MLA_V = 64
ROPE_THETA = 10000.0
Q_BLOCK = 128
GLA_HEADS = 4
GLA_DK = D_MODEL // 2 // GLA_HEADS
GLA_DV = D_MODEL // GLA_HEADS
GLA_GATE_RANK = 16
GLA_TAU = 16.0
GLA_CHUNK = 64
PEER_HEADS = 8
PEER_NKEYS = 128
PEER_EXPERTS = PEER_NKEYS * PEER_NKEYS
PEER_QDIM = 128
PEER_HALF = PEER_QDIM // 2
PEER_TOPK = 16
PEER_BLOCK = 128
NORM_EPS = 1e-6
N_MLA = (DEPTH + 1) // 2
N_GLA = DEPTH // 2


def rms_norm(x, gain):
    xf = x.astype(jnp.float32)
    y = xf * lax.rsqrt(jnp.mean(xf * xf, axis=-1, keepdims=True) + NORM_EPS)
    return (y * gain.astype(jnp.float32)).astype(x.dtype)

def apply_rope(x, positions):
    half = x.shape[-1] // 2
    inv_freq = ROPE_THETA ** (-jnp.arange(half, dtype=jnp.float32) / half)
    ang = positions.astype(jnp.float32)[..., None] * inv_freq
    cos = jnp.cos(ang)[:, :, None, :]
    sin = jnp.sin(ang)[:, :, None, :]
    x1 = x[..., :half].astype(jnp.float32)
    x2 = x[..., half:].astype(jnp.float32)
    out = jnp.concatenate([x1 * cos - x2 * sin, x2 * cos + x1 * sin], axis=-1)
    return out.astype(x.dtype)

def causal_attention(q, k, v):
    B, S, H, Dqk = q.shape
    Dv = v.shape[-1]
    nb = S // Q_BLOCK
    scale = Dqk ** -0.5
    kh = k.transpose(0, 2, 1, 3)
    vh = v.transpose(0, 2, 1, 3)
    qb = q.reshape(B, nb, Q_BLOCK, H, Dqk).transpose(1, 0, 3, 2, 4)
    key_idx = jnp.arange(S)

    def one_block(args):
        qi, blk = args
        s = jnp.einsum('bhqd,bhkd->bhqk', qi, kh).astype(jnp.float32) * scale
        q_idx = blk * Q_BLOCK + jnp.arange(Q_BLOCK)
        mask = key_idx[None, :] <= q_idx[:, None]
        s = jnp.where(mask, s, -jnp.inf)
        p = jax.nn.softmax(s, axis=-1).astype(vh.dtype)
        return jnp.einsum('bhqk,bhkd->bhqd', p, vh)

    o = lax.map(one_block, (qb, jnp.arange(nb)))
    return o.transpose(1, 0, 3, 2, 4).reshape(B, S, H, Dv)

def mla_mixer(x, positions, w_down, g_q_lat, w_uq, g_kv_lat, w_ukv, g_qn, g_kn, w_o):
    B, S, _ = x.shape
    down = x @ w_down
    c_q = rms_norm(down[..., :MLA_Q_RANK], g_q_lat)
    c_kv = rms_norm(down[..., MLA_Q_RANK:MLA_Q_RANK + MLA_KV_RANK], g_kv_lat)
    k_rope = down[..., MLA_Q_RANK + MLA_KV_RANK:]
    q = (c_q @ w_uq).reshape(B, S, MLA_HEADS, MLA_QK)
    kv = (c_kv @ w_ukv).reshape(B, S, MLA_HEADS, MLA_NOPE + MLA_V)
    k = jnp.concatenate([kv[..., :MLA_NOPE],
                         jnp.broadcast_to(k_rope[:, :, None, :], (B, S, MLA_HEADS, MLA_ROPE))], axis=-1)
    v = kv[..., MLA_NOPE:]
    q = rms_norm(q, g_qn)
    k = rms_norm(k, g_kn)
    q = jnp.concatenate([q[..., :MLA_NOPE], apply_rope(q[..., MLA_NOPE:], positions)], axis=-1)
    k = jnp.concatenate([k[..., :MLA_NOPE], apply_rope(k[..., MLA_NOPE:], positions)], axis=-1)
    o = causal_attention(q, k, v)
    return o.reshape(B, S, MLA_HEADS * MLA_V) @ w_o

def chunked_gla(q, k, v, log_a):
    B, S, H, DK = q.shape
    DV = v.shape[-1]
    C = GLA_CHUNK
    n = S // C

    def to_chunks(t):
        return t.astype(jnp.float32).reshape(B, n, C, H, t.shape[-1]).transpose(1, 0, 3, 2, 4)

    qc, kc, vc, gc = to_chunks(q), to_chunks(k), to_chunks(v), to_chunks(log_a)
    b = jnp.cumsum(gc, axis=3)
    b_last = b[..., -1:, :]
    q_dec = qc * jnp.exp(b)
    k_inv = kc * jnp.exp(-b)
    causal = jnp.tril(jnp.ones((C, C), dtype=bool))
    attn = jnp.where(causal, jnp.einsum('nbhtk,nbhsk->nbhts', q_dec, k_inv), 0.0)
    o_intra = jnp.einsum('nbhts,nbhsv->nbhtv', attn, vc)
    kv_chunk = jnp.einsum('nbhsk,nbhsv->nbhkv', kc * jnp.exp(b_last - b), vc)
    chunk_decay = jnp.exp(b_last[..., 0, :])

    def step(state, inp):
        qd, kv, dec = inp
        o = jnp.einsum('bhtk,bhkv->bhtv', qd, state)
        return state * dec[..., None] + kv, o

    state0 = jnp.zeros((B, H, DK, DV), jnp.float32)
    _, o_inter = lax.scan(step, state0, (q_dec, kv_chunk, chunk_decay))
    o = o_intra + o_inter
    return o.transpose(1, 0, 3, 2, 4).reshape(B, S, H, DV)

def gla_mixer(x, w_in, w_g2, b_g, g_on, w_o):
    B, S, _ = x.shape
    HK = GLA_HEADS * GLA_DK
    HV = GLA_HEADS * GLA_DV
    proj = x @ w_in
    q = proj[..., :HK].reshape(B, S, GLA_HEADS, GLA_DK) * (GLA_DK ** -0.5)
    k = proj[..., HK:2 * HK].reshape(B, S, GLA_HEADS, GLA_DK)
    v = proj[..., 2 * HK:2 * HK + HV].reshape(B, S, GLA_HEADS, GLA_DV)
    r = proj[..., 2 * HK + HV:2 * HK + 2 * HV]
    g_low = proj[..., 2 * HK + 2 * HV:]
    log_a = jax.nn.log_sigmoid((g_low @ w_g2 + b_g).astype(jnp.float32)) / GLA_TAU
    log_a = log_a.reshape(B, S, GLA_HEADS, GLA_DK)
    o = chunked_gla(q, k, v, log_a)
    o = rms_norm(o, g_on).reshape(B, S, HV).astype(x.dtype)
    return (o * jax.nn.silu(r)) @ w_o

def peer_ffn(x, w_query, sub_keys, u_tab, v_tab):
    B, S, D = x.shape
    T = PEER_BLOCK
    nb = S // T
    xb = x.reshape(B, nb, T, D).transpose(1, 0, 2, 3)

    def one_block(xi):
        q = (xi @ w_query).reshape(B, T, PEER_HEADS, 2, PEER_HALF)
        s = jnp.einsum('bthcd,cnd->bthcn', q, sub_keys).astype(jnp.float32)
        s_top, i_top = lax.top_k(s, PEER_TOPK)
        cand = s_top[..., 0, :, None] + s_top[..., 1, None, :]
        cand_idx = i_top[..., 0, :, None] * PEER_NKEYS + i_top[..., 1, None, :]
        best, pos = lax.top_k(cand.reshape(B, T, PEER_HEADS, PEER_TOPK * PEER_TOPK), PEER_TOPK)
        idx = jnp.take_along_axis(cand_idx.reshape(B, T, PEER_HEADS, PEER_TOPK * PEER_TOPK), pos, axis=-1)
        gate = jax.nn.softmax(best, axis=-1)
        u = u_tab[idx]
        h = jax.nn.gelu(jnp.einsum('bthkd,btd->bthk', u, xi).astype(jnp.float32), approximate=False)
        w = (gate * h).astype(xi.dtype)
        return jnp.einsum('bthk,bthkd->btd', w, v_tab[idx])

    out = lax.map(one_block, xb)
    return out.transpose(1, 0, 2, 3).reshape(B, S, D)

def first_inputs(seed: int = 0) -> dict:
    key = jax.random.key(seed)
    ks = jax.random.split(key, 24)

    def normal(k, shape, scale):
        return jax.random.normal(k, shape, jnp.float32) * scale

    def gain(k, shape):
        return 1.0 + 0.02 * jax.random.normal(k, shape, jnp.float32)

    D = D_MODEL
    HK = GLA_HEADS * GLA_DK
    HV = GLA_HEADS * GLA_DV
    x = jax.random.normal(ks[0], (BATCH, SEQ, D), jnp.float32)
    offsets = jax.random.randint(ks[1], (BATCH, 1), 0, 4096, dtype=jnp.int32)
    positions = (offsets + jnp.arange(SEQ, dtype=jnp.int32)[None, :]).astype(jnp.int32)
    return {
        "x": x,
        "positions": positions,
        "attn_norm_g": gain(ks[2], (DEPTH, D)),
        "ffn_norm_g": gain(ks[3], (DEPTH, D)),
        "mla_w_down": normal(ks[4], (N_MLA, D, MLA_Q_RANK + MLA_KV_RANK + MLA_ROPE), D ** -0.5),
        "mla_g_q_lat": gain(ks[5], (N_MLA, MLA_Q_RANK)),
        "mla_w_uq": normal(ks[6], (N_MLA, MLA_Q_RANK, MLA_HEADS * MLA_QK), MLA_Q_RANK ** -0.5),
        "mla_g_kv_lat": gain(ks[7], (N_MLA, MLA_KV_RANK)),
        "mla_w_ukv": normal(ks[8], (N_MLA, MLA_KV_RANK, MLA_HEADS * (MLA_NOPE + MLA_V)), MLA_KV_RANK ** -0.5),
        "mla_g_qn": gain(ks[9], (N_MLA, MLA_QK)),
        "mla_g_kn": gain(ks[10], (N_MLA, MLA_QK)),
        "mla_w_o": normal(ks[11], (N_MLA, MLA_HEADS * MLA_V, D), (MLA_HEADS * MLA_V) ** -0.5),
        "gla_w_in": normal(ks[12], (N_GLA, D, 2 * HK + 2 * HV + GLA_GATE_RANK), D ** -0.5),
        "gla_w_g2": normal(ks[13], (N_GLA, GLA_GATE_RANK, HK), GLA_GATE_RANK ** -0.5),
        "gla_b_g": normal(ks[14], (N_GLA, HK), 0.02),
        "gla_g_on": gain(ks[15], (N_GLA, GLA_DV)),
        "gla_w_o": normal(ks[16], (N_GLA, HV, D), HV ** -0.5),
        "peer_w_query": normal(ks[17], (DEPTH, D, PEER_HEADS * PEER_QDIM), D ** -0.5),
        "peer_sub_keys": normal(ks[18], (DEPTH, 2, PEER_NKEYS, PEER_HALF), PEER_HALF ** -0.5),
        "peer_u": normal(ks[19], (DEPTH, PEER_EXPERTS, D), D ** -0.5),
        "peer_v": normal(ks[20], (DEPTH, PEER_EXPERTS, D), 0.5 * PEER_HEADS ** -0.5),
    }

def first_block(x, positions, attn_norm_g, ffn_norm_g, mla_w_down, mla_g_q_lat, mla_w_uq, mla_g_kv_lat,
              mla_w_ukv, mla_g_qn, mla_g_kn, mla_w_o, gla_w_in, gla_w_g2, gla_b_g, gla_g_on, gla_w_o,
              peer_w_query, peer_sub_keys, peer_u, peer_v):
    h = x
    for i in range(DEPTH):
        hn = rms_norm(h, attn_norm_g[i])
        j = i // 2
        if i % 2 == 0:
            mix = mla_mixer(hn, positions, mla_w_down[j], mla_g_q_lat[j], mla_w_uq[j], mla_g_kv_lat[j],
                            mla_w_ukv[j], mla_g_qn[j], mla_g_kn[j], mla_w_o[j])
        else:
            mix = gla_mixer(hn, gla_w_in[j], gla_w_g2[j], gla_b_g[j], gla_g_on[j], gla_w_o[j])
        h = h + mix
        h = h + peer_ffn(rms_norm(h, ffn_norm_g[i]), peer_w_query[i], peer_sub_keys[i], peer_u[i], peer_v[i])
    return h


DEPTH_2 = 1

HEAD_DIM = 64
GRID_W = 64
NA_HEADS = 8
NA_KH_MAX = 8
NA_KW = 16
NA_QCB = NA_KW
NA_SPAN = 2 * NA_KW
SW_HEADS = 8
SW_KV_HEADS = 2
SW_WINDOW = 128
SW_BLOCK = 128
T5_BUCKETS = 32
T5_MAX_DIST = 128
FFN_HIDDEN = -(-8 * D_MODEL // (3 * 256)) * 256

A_W = NA_HEADS * HEAD_DIM
B_QW = SW_HEADS * HEAD_DIM
B_KVW = SW_KV_HEADS * HEAD_DIM
IN_WIDTHS = [A_W, A_W, A_W, B_QW, B_KVW, B_KVW, D_MODEL, D_MODEL]
IN_WIDTH = sum(IN_WIDTHS)
IN_SPLITS = list(np.cumsum(IN_WIDTHS)[:-1])
RMS_EPS = 1e-6
NEG_INF = -1e30


def rms_norm_2(x, g):
    xf = x.astype(jnp.float32)
    y = xf * lax.rsqrt(jnp.mean(xf * xf, axis=-1, keepdims=True) + RMS_EPS)
    return y.astype(x.dtype) * g

def t5_bucket(rel):
    half = T5_BUCKETS // 2
    max_exact = half // 2
    ret = (rel > 0).astype(np.int32) * half
    n = np.abs(rel)
    large = max_exact + (np.log(np.maximum(n, 1) / max_exact)
                         / np.log(T5_MAX_DIST / max_exact) * (half - max_exact)).astype(np.int32)
    large = np.minimum(large, half - 1)
    return ret + np.where(n < max_exact, n, large)

def neighbourhood_attention(q, k, v, rpb):
    B, T, H, D = q.shape
    rows = T // GRID_W
    kh = min(NA_KH_MAX, rows)
    ncb = GRID_W // NA_QCB
    r = np.arange(rows)
    row_start = np.clip(r - kh // 2, 0, rows - kh)
    key_rows = row_start[:, None] + np.arange(kh)[None, :]
    j = np.arange(ncb)
    span_start = np.clip(j * NA_QCB - NA_KW // 2, 0, GRID_W - NA_SPAN)
    key_cols = span_start[:, None] + np.arange(NA_SPAN)[None, :]
    q_cols = j[:, None] * NA_QCB + np.arange(NA_QCB)[None, :]
    win_start = np.clip(q_cols - NA_KW // 2, 0, GRID_W - NA_KW)
    kc = key_cols[:, None, :]
    in_win = (kc >= win_start[..., None]) & (kc < win_start[..., None] + NA_KW)

    idx = (key_rows[:, None, :, None] * GRID_W + key_cols[None, :, None, :]).reshape(rows, ncb, kh * NA_SPAN)
    kg = jnp.take(k, idx, axis=1)
    vg = jnp.take(v, idx, axis=1)
    qb = q.reshape(B, rows, ncb, NA_QCB, H, D)
    s = jnp.einsum('brjqhd,brjkhd->brjhqk', qb, kg,
                   preferred_element_type=jnp.float32) * (HEAD_DIM ** -0.5)

    dr = key_rows - r[:, None] + (NA_KH_MAX - 1)
    dc = np.clip(kc - q_cols[..., None], -(NA_KW - 1), NA_KW - 1) + (NA_KW - 1)
    bias = rpb[dr[:, None, None, :, None], dc[None, :, :, None, :]]
    bias = jnp.transpose(bias, (0, 1, 5, 2, 3, 4)).astype(jnp.float32)
    bias = jnp.where(in_win[None, :, None, :, None, :], bias, NEG_INF)
    bias = bias.reshape(rows, ncb, H, NA_QCB, kh * NA_SPAN)
    p = jax.nn.softmax(s + bias[None], axis=-1)
    o = jnp.einsum('brjhqk,brjkhd->brjqhd', p.astype(v.dtype), vg)
    return o.reshape(B, T, H, D)

def sliding_window_attention(q, k, v, sink, t5_table):
    B, T, H, D = q.shape
    kvh = k.shape[2]
    g = H // kvh
    nb = T // SW_BLOCK
    pad = ((0, 0), (SW_BLOCK, SW_BLOCK), (0, 0), (0, 0))
    kp = jnp.pad(k, pad).reshape(B, nb + 2, SW_BLOCK, kvh, D)
    vp = jnp.pad(v, pad).reshape(B, nb + 2, SW_BLOCK, kvh, D)
    kw = jnp.concatenate([kp[:, :-2], kp[:, 1:-1], kp[:, 2:]], axis=2)
    vw = jnp.concatenate([vp[:, :-2], vp[:, 1:-1], vp[:, 2:]], axis=2)
    qb = q.reshape(B, nb, SW_BLOCK, kvh, g, D)
    s = jnp.einsum('bnqkgd,bnskd->bnkgqs', qb, kw,
                   preferred_element_type=jnp.float32) * (HEAD_DIM ** -0.5)

    rel = np.arange(3 * SW_BLOCK)[None, :] - SW_BLOCK - np.arange(SW_BLOCK)[:, None]
    bias = t5_table[t5_bucket(rel)]
    bias = jnp.transpose(bias, (2, 0, 1)).reshape(kvh, g, SW_BLOCK, 3 * SW_BLOCK).astype(jnp.float32)
    key_pos = np.arange(nb)[:, None] * SW_BLOCK + np.arange(3 * SW_BLOCK)[None, :] - SW_BLOCK
    valid = (np.abs(rel) <= SW_WINDOW)[None] & ((key_pos >= 0) & (key_pos < T))[:, None, :]
    s = jnp.where(valid[None, :, None, None], s + bias[None, None], NEG_INF)

    sk = sink.astype(jnp.float32).reshape(1, 1, kvh, g, 1, 1)
    m = jnp.maximum(jnp.max(s, axis=-1, keepdims=True), sk)
    e = jnp.exp(s - m)
    p = e / (jnp.sum(e, axis=-1, keepdims=True) + jnp.exp(sk - m))
    o = jnp.einsum('bnkgqs,bnskd->bnqkgd', p.astype(v.dtype), vw)
    return o.reshape(B, T, H, D)

def second_inputs(seed: int = 0) -> dict:
    key = jax.random.key(seed)
    ks = jax.random.split(key, 18)
    f32 = jnp.float32

    def w(k, shape, fan_in):
        return jax.random.normal(k, shape, f32) * fan_in ** -0.5

    def gain(k, shape):
        return 1.0 + 0.05 * jax.random.normal(k, shape, f32)

    return {
        "x": jax.random.normal(ks[0], (BATCH, SEQ, D_MODEL), f32),
        "norm_mix": gain(ks[1], (DEPTH_2, D_MODEL)),
        "w_in": w(ks[2], (DEPTH_2, D_MODEL, IN_WIDTH), D_MODEL),
        "q_norm_a": gain(ks[3], (DEPTH_2, HEAD_DIM)),
        "k_norm_a": gain(ks[4], (DEPTH_2, HEAD_DIM)),
        "rpb_a": 0.1 * jax.random.normal(ks[5], (DEPTH_2, 2 * NA_KH_MAX - 1, 2 * NA_KW - 1, NA_HEADS), f32),
        "q_norm_b": gain(ks[6], (DEPTH_2, HEAD_DIM)),
        "k_norm_b": gain(ks[7], (DEPTH_2, HEAD_DIM)),
        "sink_b": 1.0 + 0.5 * jax.random.normal(ks[8], (DEPTH_2, SW_HEADS), f32),
        "t5_table": 0.1 * jax.random.normal(ks[9], (T5_BUCKETS, SW_HEADS), f32),
        "w_branch_a": w(ks[10], (DEPTH_2, A_W, D_MODEL), A_W),
        "w_branch_b": w(ks[11], (DEPTH_2, B_QW, D_MODEL), B_QW),
        "w_out": w(ks[12], (DEPTH_2, D_MODEL, D_MODEL), D_MODEL),
        "norm_ffn": gain(ks[13], (DEPTH_2, D_MODEL)),
        "w_gate": w(ks[14], (DEPTH_2, D_MODEL, FFN_HIDDEN), D_MODEL),
        "w_up": w(ks[15], (DEPTH_2, D_MODEL, FFN_HIDDEN), D_MODEL),
        "w_down": w(ks[16], (DEPTH_2, FFN_HIDDEN, D_MODEL), FFN_HIDDEN),
    }

def second_block(x, norm_mix, w_in, q_norm_a, k_norm_a, rpb_a, q_norm_b, k_norm_b, sink_b,
              t5_table, w_branch_a, w_branch_b, w_out, norm_ffn, w_gate, w_up, w_down):
    B, T, _ = x.shape
    for l in range(DEPTH_2):
        h = rms_norm_2(x, norm_mix[l])
        proj = jnp.einsum('btd,de->bte', h, w_in[l])
        q_a, k_a, v_a, q_b, k_b, v_b, g_a, g_b = jnp.split(proj, IN_SPLITS, axis=-1)

        q_a = rms_norm_2(q_a.reshape(B, T, NA_HEADS, HEAD_DIM), q_norm_a[l])
        k_a = rms_norm_2(k_a.reshape(B, T, NA_HEADS, HEAD_DIM), k_norm_a[l])
        v_a = v_a.reshape(B, T, NA_HEADS, HEAD_DIM)
        o_a = neighbourhood_attention(q_a, k_a, v_a, rpb_a[l]).reshape(B, T, A_W)

        q_b = rms_norm_2(q_b.reshape(B, T, SW_HEADS, HEAD_DIM), q_norm_b[l])
        k_b = rms_norm_2(k_b.reshape(B, T, SW_KV_HEADS, HEAD_DIM), k_norm_b[l])
        v_b = v_b.reshape(B, T, SW_KV_HEADS, HEAD_DIM)
        o_b = sliding_window_attention(q_b, k_b, v_b, sink_b[l], t5_table).reshape(B, T, B_QW)

        y = (jax.nn.sigmoid(g_a) * jnp.einsum('bte,ed->btd', o_a, w_branch_a[l])
             + jax.nn.sigmoid(g_b) * jnp.einsum('bte,ed->btd', o_b, w_branch_b[l]))
        x = x + jnp.einsum('btd,de->bte', y, w_out[l])

        h = rms_norm_2(x, norm_ffn[l])
        u = jax.nn.silu(jnp.einsum('btd,df->btf', h, w_gate[l])) * jnp.einsum('btd,df->btf', h, w_up[l])
        x = x + jnp.einsum('btf,fd->btd', u, w_down[l])
    return x


def setup_inputs(seed=0):
    out = dict(first_inputs(seed))
    for name, value in second_inputs(seed + 1).items():
        if name != "x":
            out[name + "_2"] = value
    return out


def reference(
    x, positions, attn_norm_g, ffn_norm_g, mla_w_down, mla_g_q_lat, mla_w_uq, mla_g_kv_lat,
    mla_w_ukv, mla_g_qn, mla_g_kn, mla_w_o, gla_w_in, gla_w_g2, gla_b_g, gla_g_on, gla_w_o,
    peer_w_query, peer_sub_keys, peer_u, peer_v, norm_mix_2, w_in_2, q_norm_a_2, k_norm_a_2,
    rpb_a_2, q_norm_b_2, k_norm_b_2, sink_b_2, t5_table_2, w_branch_a_2, w_branch_b_2, w_out_2,
    norm_ffn_2, w_gate_2, w_up_2, w_down_2,
):
    x = first_block(
        x, positions, attn_norm_g, ffn_norm_g, mla_w_down, mla_g_q_lat, mla_w_uq, mla_g_kv_lat,
        mla_w_ukv, mla_g_qn, mla_g_kn, mla_w_o, gla_w_in, gla_w_g2, gla_b_g, gla_g_on, gla_w_o,
        peer_w_query, peer_sub_keys, peer_u, peer_v,
    )
    return second_block(
        x, norm_mix_2, w_in_2, q_norm_a_2, k_norm_a_2, rpb_a_2, q_norm_b_2, k_norm_b_2,
        sink_b_2, t5_table_2, w_branch_a_2, w_branch_b_2, w_out_2, norm_ffn_2, w_gate_2, w_up_2,
        w_down_2,
    )


_drawn_inputs = setup_inputs


def setup_inputs(seed=0):
    import zlib

    import numpy as np

    out = dict(_drawn_inputs(seed))
    spreads = {}
    factors = {'mla_g_q_lat': 4.129,
     'mla_g_kv_lat': 3.557,
     'mla_g_qn': 4.443,
     'mla_g_kn': 4.407,
     'gla_b_g': 7.463,
     'gla_g_on': 4.278,
     'norm_mix_2': 5.561,
     'q_norm_a_2': 8.0,
     'k_norm_a_2': 8.0,
     'rpb_a_2': 6.506,
     'q_norm_b_2': 8.0,
     'k_norm_b_2': 8.0,
     'sink_b_2': 8.0,
     't5_table_2': 8.0,
     'norm_ffn_2': 8.0}
    for name, (base, spread) in spreads.items():
        noise = np.random.default_rng([zlib.crc32(name.encode()), seed]).standard_normal(out[name].shape)
        drawn = base * np.exp(spread * noise) if base else spread * noise
        out[name] = __import__('jax').numpy.asarray(drawn.astype(out[name].dtype))
    for name, factor in factors.items():
        out[name] = (out[name] * factor).astype(out[name].dtype)
    return out
```

```python
import math
from contextlib import ExitStack

import numpy as np

import concourse.bass as bass
from concourse import mybir

ALU = mybir.AluOpType
ACT = mybir.ActivationFunctionType
AX_X = mybir.AxisListType.X
F32 = mybir.dt.float32
F32R = mybir.dt.float32r
I32 = mybir.dt.int32
U32 = mybir.dt.uint32

P = 128
D = 1024
KD = D // P
T = 256
NT = T // P
EPS = 1e-6

H_MLA, NOPE, ROPE, DV = 16, 64, 32, 64
QK = NOPE + ROPE
HALF = ROPE // 2
R_Q, R_KV = 384, 256
W_DOWN = R_Q + R_KV + ROPE

H_G, DK_G, DV_G, R_G, TAU, CH = 4, 128, 256, 16, 16.0, 64
NCH = T // CH
G_Q, G_K, G_V, G_R, G_LOW = 0, 512, 1024, 2048, 3072
W_GLA = G_LOW + R_G

H_P, NK, TOPK = 8, 128, 16
SLOTS = H_P * TOPK

DH, H_A, H_B, KV_B = 64, 8, 8, 2
A_W = H_A * DH
A_Q, A_K, A_V, B_Q, B_K, B_V, GATE_A, GATE_B = 0, 512, 1024, 1536, 2048, 2176, 2304, 3328
W_IN2 = 4352
FFN = 2816
NFT = FFN // P

NEG = -1e30

COLS = {}
_at = 0
for _name, _n in (("attn0", KD), ("attn1", KD), ("ffn0", KD), ("ffn1", KD), ("mix2", KD), ("ffn2", KD),
                  ("q_lat", R_Q // P), ("kv_lat", R_KV // P), ("b_g", H_G), ("one", KD), ("eps", 1)):
    COLS[_name] = (_at, _n)
    _at += _n
N_COLS = _at

ROWS = {}
_at = 0
for _name, _n in (("qn", QK), ("kn", QK), ("on", DV_G), ("qa", DH), ("ka", DH), ("qb", DH), ("kb", DH),
                  ("sink", H_B), ("freq", HALF)):
    ROWS[_name] = (_at, _n)
    _at += _n
N_ROWS = _at


class Signal:

    def __init__(self, sem):
        self.sem, self.base = sem, 0

    def at(self, n):
        return n + self.base

    def advance(self, n):
        self.base += n


class Chain:

    def __init__(self, sem):
        self.sem, self.count = sem, 0

    def link(self, eng, ins):
        self.count += 1
        ins.then_inc(self.sem, 1)
        eng.wait_ge(self.sem, self.count)


class Kernel:
    def __init__(self, nc, ctx, dram):
        self.nc, self.ctx, self.dram = nc, ctx, dram
        self.signals, self.named = {}, {}
        self.bank = [ctx.enter_context(nc.psum_tensor(f"bank{i}", [P, 512], F32)) for i in range(8)]
        self.act_chain = Chain(ctx.enter_context(nc.semaphore("act_chain")))
        self.dve_chain = Chain(ctx.enter_context(nc.semaphore("dve_chain")))
        self.pool_chain = Chain(ctx.enter_context(nc.semaphore("pool_chain")))
        self.ident = self.sb(ctx, "ident", [P, P])
        self.cols = self.sb(ctx, "cols", [P, N_COLS])
        self.rows = self.sb(ctx, "rows", [P, N_ROWS])
        self.h = self.sb(ctx, "h", [P, NT, D])
        self.xh = self.sb(ctx, "xh", [P, KD, T], F32R)
        self.xl = self.sb(ctx, "xl", [P, KD, T], F32R)

    def sb(self, ctx, name, shape, dt=F32):
        self.named[name] = self.named.get(name, 0) + 1
        return ctx.enter_context(self.nc.sbuf_tensor(f"{name}_{self.named[name]}", shape, dt))

    def sig(self, name):
        if name not in self.signals:
            self.signals[name] = Signal(self.ctx.enter_context(self.nc.semaphore(name)))
        return self.signals[name]

    def col(self, name):
        a, n = COLS[name]
        return self.cols[:, a:a + n]

    def row(self, name):
        a, n = ROWS[name]
        return self.rows[:, a:a + n]


def setup(k):
    loaded, built = k.sig("setup_loaded"), k.sig("setup_built")
    with k.nc.Block() as block:

        @block.sync
        def _(sp):
            sp.dma_start(k.h[:], k.dram["x"].rearrange("(a p) d -> p a d", p=P)).then_inc(loaded.sem, 16)
            sp.dma_start(k.cols[:], k.dram["cols"]).then_inc(loaded.sem, 16)
            sp.dma_start(k.rows[:], k.dram["rows"]).then_inc(loaded.sem, 16)
            sp.wait_ge(loaded.sem, 48)

        @block.gpsimd
        def _(pool):
            pool.memset(k.ident[:], 0.0).then_inc(built.sem, 1)
            pool.wait_ge(built.sem, 1)
            pool.affine_select(out=k.ident[:], in_=k.ident[:], compare_op=ALU.not_equal, fill=1.0, base=0,
                               pattern=[[-1, P]], channel_multiplier=1).then_inc(built.sem, 1)
            pool.wait_ge(built.sem, 2)


def transposes(k, name, jobs, before_act=None, before_dve=None, act_ready=0, dve_ready=0):
    turned, act_out, dve_out = k.sig("tr_turned"), k.sig("tr_act_out"), k.sig("tr_dve_out")
    prepared = k.sig("tr_prepared")
    nb = 4
    acts = [sum(j[1] is not None for j in jobs[:n]) for n in range(len(jobs) + 1)]
    dves = [sum(j[2] is not None for j in jobs[:n]) for n in range(len(jobs) + 1)]
    with k.nc.Block() as block:

        @block.scalar
        def _(act):
            if before_act:
                before_act(act)
            for n, (_, act_copy, _) in enumerate(jobs):
                if act_copy:
                    act.wait_ge(turned.sem, turned.at(n + 1))
                    act_copy(act, k.bank[n % nb]).then_inc(act_out.sem, 1)

        @block.vector
        def _(dve):
            if before_dve:
                before_dve(dve, prepared)
            for n, (_, act_copy, dve_copy) in enumerate(jobs):
                if dve_copy:
                    dve.wait_ge(turned.sem, turned.at(n + 1))
                    if act_copy:
                        dve.wait_ge(act_out.sem, act_out.at(acts[n + 1]))
                    dve_copy(dve, k.bank[n % nb]).then_inc(dve_out.sem, 1)

        @block.tensor
        def _(pe):
            for n, (blocks, _, _) in enumerate(jobs):
                if dve_ready:
                    pe.wait_ge(prepared.sem, prepared.at(min(n + 1, dve_ready)))
                if n >= nb:
                    pe.wait_ge(act_out.sem, act_out.at(acts[n - nb + 1]))
                    pe.wait_ge(dve_out.sem, dve_out.at(dves[n - nb + 1]))
                for src, rows, c0 in blocks:
                    last = pe.transpose(k.bank[n % nb][0:rows, c0:c0 + P], src, k.ident[:])
                last.then_inc(turned.sem, 1)

    turned.advance(len(jobs))
    act_out.advance(acts[-1])
    dve_out.advance(dves[-1])
    prepared.advance(dve_ready)


def split_jobs(k, src, kt, xh, xl, gain):
    jobs = []
    for c in range(kt):
        blocks = [(src[:, a, c * P:(c + 1) * P], P, a * P) for a in range(NT)]

        def act_copy(act, bank, c=c):
            return act.activation(xh[:, c, :], bank[:, 0:T], ACT.Copy, scale=gain[:, c:c + 1])

        def dve_copy(dve, bank, c=c):
            return dve.scalar_tensor_tensor(out=xl[:, c, :], in0=bank[:, 0:T], scalar=gain[:, c:c + 1],
                                            in1=xh[:, c, :].bitcast(F32), op0=ALU.mult, op1=ALU.subtract)

        jobs.append((blocks, act_copy, dve_copy))
    return jobs


def norm_groups(k, groups, name):
    sq, rs, ln = k.sig("nm_squared"), k.sig("nm_summed"), k.sig("nm_rstd")
    with k.nc.Block() as block:

        @block.scalar
        def _(act):
            for n, (src, _, _, work, _) in enumerate(groups):
                act.activation(work, src, ACT.Square).then_inc(sq.sem, 1)
            for n, (src, _, _, _, sums) in enumerate(groups):
                act.wait_ge(rs.sem, rs.at(n + 1))
                k.act_chain.link(act, act.activation(sums, sums, ACT.Ln, scale=1.0 / src.shape[-1],
                                                     bias=k.col("eps")))
                act.activation(sums, sums, ACT.Exp, scale=-0.5).then_inc(ln.sem, 1)

        @block.vector
        def _(dve):
            for n, (_, _, _, work, sums) in enumerate(groups):
                dve.wait_ge(sq.sem, sq.at(n + 1))
                dve.tensor_reduce(sums, work, AX_X, ALU.add).then_inc(rs.sem, 1)
            for n, (src, out, gain, _, sums) in enumerate(groups):
                dve.wait_ge(ln.sem, ln.at(n + 1))
                shape = list(src.shape)
                k.dve_chain.link(dve, dve.tensor_tensor(out, src, sums.unsqueeze(2).broadcast_to(shape), ALU.mult))
                if gain is not None:
                    k.dve_chain.link(dve, dve.tensor_tensor(out, out, gain.unsqueeze(1).broadcast_to(shape), ALU.mult))

    for s in (sq, rs, ln):
        s.advance(len(groups))


def norm_split(k, gain):
    with ExitStack() as ctx:
        y = k.sb(ctx, "ns_y", [P, NT, D])
        s = k.sb(ctx, "ns_s", [P, NT])
        norm_groups(k, [(k.h[:], y[:], None, y[:], s[:])], "h")
        transposes(k, "h", split_jobs(k, y, KD, k.xh, k.xl, k.col(gain)))


def gemm(k, xh, xl, kt, w, n_out, width, out, add=False):
    blk = 4 if kt % 4 == 0 else kt
    per = kt // blk
    chunks = n_out // width
    assert chunks * width == n_out and width <= 512
    loaded = [k.sig(f"gm_loaded{s}") for s in range(2)]
    hi, lo, used = k.sig("gm_hi"), k.sig("gm_lo"), k.sig("gm_used")
    act_freed, dve_freed = k.sig("gm_act_freed"), k.sig("gm_dve_freed")
    pairs = (chunks - 1) // 2 if chunks > 4 else 0
    with ExitStack() as ctx:
        raw = k.sb(ctx, "gm_raw", [P, 2, blk, width])
        wh = k.sb(ctx, "gm_wh", [P, 2, width], F32R)
        wl = k.sb(ctx, "gm_wl", [P, 2, width], F32R)

        def chunked(eng, body, after=None):
            body(0, 0)
            if pairs:
                with eng.Fori(0, pairs) as m:
                    body(2 * m + 1, 1)
                    body(2 * m + 2, 2)
            for c in range(1 + 2 * pairs, chunks):
                body(c, c)
            if after:
                after()

        with k.nc.Block() as block:

            @block.sync
            def _(sp):
                def body(c, like):
                    for b in range(per):
                        n, slot = c * per + b, (like * per + b) % 2
                        if not (isinstance(n, int) and n < 2):
                            sp.wait_ge(lo.sem, lo.at((n - 1) * blk))
                        sp.dma_start(raw[:, slot, :, :],
                                     w[b * blk * P:(b + 1) * blk * P, bass.ds(c * width, width)]
                                     .rearrange("(k p) n -> p k n", p=P)).then_inc(loaded[slot].sem, 16)
                chunked(sp, body)

            def arrived(eng, c, like, b):
                n, slot = c * per + b, (like * per + b) % 2
                eng.wait_ge(loaded[slot].sem, loaded[slot].at((n - slot) * 8 + 16))

            @block.scalar
            def _(act):
                def evacuate(c, like):
                    if not add:
                        act.wait_ge(used.sem, used.at((c + 1) * kt))
                        act.activation(out[:, 0, bass.ds(c * width, width)], k.bank[2 * (like % 2)][:, 0:width],
                                       ACT.Copy).then_inc(act_freed.sem, 1)

                def body(c, like):
                    for u in range(kt):
                        if u % blk == 0:
                            arrived(act, c, like, u // blk)
                        n, slot = c * kt + u, (like * kt + u) % 2
                        if not (isinstance(n, int) and n < 2):
                            act.wait_ge(used.sem, used.at(n - 1))
                        act.activation(wh[:, slot, :], raw[:, (like * per + u // blk) % 2, u % blk, :],
                                       ACT.Copy).then_inc(hi.sem, 1)
                        if u == 1 and not (isinstance(c, int) and c == 0):
                            evacuate(c - 1, like - 1)
                chunked(act, body, lambda: evacuate(chunks - 1, chunks - 1))

            @block.vector
            def _(dve):
                def evacuate(c, like):
                    dve.wait_ge(used.sem, used.at((c + 1) * kt))
                    if add:
                        for a in range(NT):
                            o = out[:, a, bass.ds(c * width, width)]
                            dve.tensor_tensor(o, o, k.bank[2 * (like % 2) + a][:, 0:width], ALU.add)\
                               .then_inc(dve_freed.sem, 1)
                    else:
                        dve.tensor_copy(out[:, 1, bass.ds(c * width, width)],
                                        k.bank[2 * (like % 2) + 1][:, 0:width]).then_inc(dve_freed.sem, 1)

                def body(c, like):
                    for u in range(kt):
                        n, slot = c * kt + u, (like * kt + u) % 2
                        dve.wait_ge(hi.sem, hi.at(n + 1))
                        dve.tensor_tensor(wl[:, slot, :], raw[:, (like * per + u // blk) % 2, u % blk, :],
                                          wh[:, slot, :].bitcast(F32), ALU.subtract).then_inc(lo.sem, 1)
                        if u == 1 and not (isinstance(c, int) and c == 0):
                            evacuate(c - 1, like - 1)
                chunked(dve, body, lambda: evacuate(chunks - 1, chunks - 1))

            @block.tensor
            def _(pe):
                def body(c, like):
                    if not (isinstance(c, int) and c < 2):
                        pe.wait_ge(dve_freed.sem, dve_freed.at((c - 1) * (2 if add else 1)))
                        if not add:
                            pe.wait_ge(act_freed.sem, act_freed.at(c - 1))
                    for u in range(kt):
                        n, slot = c * kt + u, (like * kt + u) % 2
                        pe.wait_ge(hi.sem, hi.at(n + 1))
                        ps = [k.bank[2 * (like % 2) + a][:, 0:width] for a in range(NT)]
                        for x in (xh, xl):
                            for a in range(NT):
                                pe.matmul(ps[a], x[:, u, a * P:(a + 1) * P], wh[:, slot, :],
                                          start=(u == 0 and x is xh), stop=False)
                        pe.wait_ge(lo.sem, lo.at(n + 1))
                        for a in range(NT):
                            last = pe.matmul(ps[a], xh[:, u, a * P:(a + 1) * P], wl[:, slot, :],
                                             start=False, stop=(u == kt - 1))
                        last.then_inc(used.sem, 1)
                chunked(pe, body)

    for s in (hi, lo, used):
        s.advance(chunks * kt)
    dve_freed.advance(chunks * (2 if add else 1))
    act_freed.advance(0 if add else chunks)
    blocks = chunks * per
    loaded[0].advance(16 * ((blocks + 1) // 2))
    loaded[1].advance(16 * (blocks // 2))


def narrow_gemm(k, w, c0, width, out):
    loaded, done = k.sig("nw_loaded"), k.sig("nw_done")
    with ExitStack() as ctx:
        raw = k.sb(ctx, "nw_raw", [P, KD, width])
        x = k.sb(ctx, "nw_x", [P, KD, T])
        with k.nc.Block() as block:

            @block.sync
            def _(sp):
                with k.nc.allow_non_contiguous_dma(reason="a few columns"):
                    sp.dma_start(raw[:], w[:, c0:c0 + width].rearrange("(k p) n -> p k n", p=P))\
                      .then_inc(loaded.sem, 16)

            @block.vector
            def _(dve):
                dve.tensor_tensor(x[:], k.xh[:].bitcast(F32), k.xl[:].bitcast(F32), ALU.add).then_inc(done.sem, 1)
                dve.wait_ge(done.sem, done.at(2))
                for a in range(NT):
                    k.dve_chain.link(dve, dve.tensor_copy(out[:, a, c0:c0 + width], k.bank[a][:, 0:width]))

            @block.tensor
            def _(pe):
                pe.wait_ge(loaded.sem, loaded.at(16))
                pe.wait_ge(done.sem, done.at(1))
                for u in range(KD):
                    for a in range(NT):
                        last = pe.matmul(k.bank[a][:, 0:width], x[:, u, a * P:(a + 1) * P], raw[:, u, :],
                                         start=(u == 0), stop=(u == KD - 1))
                last.then_inc(done.sem, 1)

    loaded.advance(16)
    done.advance(2)


def attention(k, heads, q_of, k_of, v_of, bias_of, scale, oh, ol, sink=None):
    scored, masked, powered, scaled = k.sig("at_scored"), k.sig("at_masked"), k.sig("at_powered"), k.sig("at_scaled")
    turned, copied, valued = k.sig("at_turned"), k.sig("at_copied"), k.sig("at_valued")
    high, low = k.sig("at_high"), k.sig("at_low")
    S, PT, O = k.bank[0:2], k.bank[2:4], k.bank[4:6]
    with ExitStack() as ctx:
        s_sb = k.sb(ctx, "at_s", [P, 2, NT, T])
        p_sb = k.sb(ctx, "at_p", [P, 2, NT, T])
        pt_sb = k.sb(ctx, "at_pt", [P, 2, NT, T])
        peak = k.sb(ctx, "at_peak", [P, 2, NT])
        npeak = k.sb(ctx, "at_npeak", [P, 2, NT])
        total = k.sb(ctx, "at_total", [P, 2, NT])
        esink = k.sb(ctx, "at_esink", [P, 2, NT])
        inv = k.sb(ctx, "at_inv", [P, 2, NT])
        pairs = heads // 2
        with k.nc.Block() as block:

            @block.tensor
            def _(pe):
                def scores(h):
                    if h >= 2:
                        pe.wait_ge(masked.sem, masked.at(h - 1))
                    for a in range(NT):
                        last = pe.matmul(S[h % 2][:, a * T:(a + 1) * T], q_of(h)[:, a * P:(a + 1) * P], k_of(h),
                                         start=True, stop=True)
                    last.then_inc(scored.sem, 1)

                scores(0)
                for h in range(heads):
                    if h + 1 < heads:
                        scores(h + 1)
                    pe.wait_ge(scaled.sem, scaled.at(h + 1))
                    if h >= 2:
                        pe.wait_ge(copied.sem, copied.at(h - 1))
                    for b in range(NT):
                        for a in range(NT):
                            last = pe.transpose(PT[h % 2][:, b * T + a * P:b * T + (a + 1) * P],
                                                p_sb[:, h % 2, a, b * P:(b + 1) * P], k.ident[:])
                    last.then_inc(turned.sem, 1)
                    pe.wait_ge(copied.sem, copied.at(h + 1))
                    if h % 2 == 0 and h >= 4:
                        pe.wait_ge(low.sem, low.at(h // 2 - 1))
                    o = O[h // 2 % 2][DV * (h % 2):DV * (h % 2) + DV, 0:T]
                    for b in range(NT):
                        last = pe.matmul(o, v_of(h, b), pt_sb[:, h % 2, b, :], start=(b == 0), stop=(b == NT - 1))
                    last.then_inc(valued.sem, 1)

            @block.vector
            def _(dve):
                def mask(h):
                    s = s_sb[:, h % 2]
                    dve.wait_ge(scored.sem, scored.at(h + 1))
                    if h >= 2:
                        dve.wait_ge(powered.sem, powered.at(h - 1))
                    dve.scalar_tensor_tensor(out=s, in0=S[h % 2][:].rearrange("p (a t) -> p a t", a=NT), scalar=scale,
                                             in1=bias_of(h), op0=ALU.mult, op1=ALU.add).then_inc(k.dve_chain.sem, 1)
                    k.dve_chain.count += 1
                    dve.wait_ge(k.dve_chain.sem, k.dve_chain.count)
                    k.dve_chain.link(dve, dve.tensor_reduce(peak[:, h % 2], s, AX_X, ALU.max))
                    if sink is not None:
                        k.dve_chain.link(dve, dve.tensor_scalar(peak[:, h % 2], peak[:, h % 2], sink[:, h:h + 1],
                                                                None, ALU.max))
                        dve.tensor_scalar(esink[:, h % 2], peak[:, h % 2], -1.0, sink[:, h:h + 1],
                                          ALU.mult, ALU.add).then_inc(k.dve_chain.sem, 1)
                        k.dve_chain.count += 1
                    k.dve_chain.link(dve, dve.tensor_scalar(npeak[:, h % 2], peak[:, h % 2], -1.0, None, ALU.mult))
                    dve.sem_inc(masked.sem, 1)

                def normalise(h):
                    dve.wait_ge(powered.sem, powered.at(h + 1))
                    if sink is not None:
                        k.dve_chain.link(dve, dve.tensor_tensor(total[:, h % 2], total[:, h % 2], esink[:, h % 2],
                                                                ALU.add))
                    k.dve_chain.link(dve, dve.reciprocal(inv[:, h % 2], total[:, h % 2]))
                    for a in range(NT):
                        last = dve.tensor_scalar(p_sb[:, h % 2, a], p_sb[:, h % 2, a], inv[:, h % 2, a:a + 1], None,
                                                 ALU.mult)
                        if a == 0:
                            last.then_inc(k.dve_chain.sem, 1)
                            k.dve_chain.count += 1
                            dve.wait_ge(k.dve_chain.sem, k.dve_chain.count)
                    last.then_inc(scaled.sem, 1)

                def low_part(c):
                    dve.wait_ge(high.sem, high.at(c + 1))
                    dve.tensor_tensor(ol[:, c, :], O[c % 2][:, 0:T], oh[:, c, :].bitcast(F32), ALU.subtract)\
                       .then_inc(low.sem, 1)

                mask(0)
                for h in range(heads):
                    if h + 1 < heads:
                        mask(h + 1)
                    if h % 2 == 0 and h >= 2:
                        low_part(h // 2 - 1)
                    normalise(h)
                low_part(pairs - 1)

            @block.scalar
            def _(act):
                def power(h):
                    act.wait_ge(masked.sem, masked.at(h + 1))
                    if h >= 2:
                        act.wait_ge(turned.sem, turned.at(h - 1))
                    if sink is not None:
                        act.activation(esink[:, h % 2], esink[:, h % 2], ACT.Exp).then_inc(k.act_chain.sem, 1)
                        k.act_chain.count += 1
                        act.wait_ge(k.act_chain.sem, k.act_chain.count)
                    for a in range(NT):
                        last = act.activation(p_sb[:, h % 2, a], s_sb[:, h % 2, a], ACT.Exp,
                                              bias=npeak[:, h % 2, a:a + 1], accum_out=total[:, h % 2, a:a + 1])
                        if a == 0:
                            k.act_chain.link(act, last)
                    last.then_inc(powered.sem, 1)

                def high_part(c):
                    act.wait_ge(valued.sem, valued.at(2 * c + 2))
                    act.activation(oh[:, c, :], O[c % 2][:, 0:T], ACT.Copy).then_inc(high.sem, 1)

                power(0)
                for h in range(heads):
                    if h + 1 < heads:
                        power(h + 1)
                    if h % 2 == 0 and h >= 2:
                        high_part(h // 2 - 1)
                    act.wait_ge(turned.sem, turned.at(h + 1))
                    if h >= 2:
                        act.wait_ge(valued.sem, valued.at(h - 1))
                    act.activation(pt_sb[:, h % 2].rearrange("p a t -> p (a t)"), PT[h % 2][:], ACT.Copy)\
                       .then_inc(copied.sem, 1)
                high_part(pairs - 1)

    for s in (scored, masked, powered, scaled, turned, copied, valued):
        s.advance(heads)
    for s in (high, low):
        s.advance(pairs)


def angles(k, cs):
    loaded, reduced, done = k.sig("ro_loaded"), k.sig("ro_reduced"), k.sig("ro_done")
    c1 = 6.28125
    c2 = float(np.float32(np.round((2 * math.pi - c1) * 2 ** 22) / 2 ** 22))
    c3 = 2 * math.pi - c1 - c2
    magic = 1.5 * 2 ** 23
    with ExitStack() as ctx:
        pos = k.sb(ctx, "ro_pos", [P, NT], I32)
        posf = k.sb(ctx, "ro_posf", [P, NT])
        ang = k.sb(ctx, "ro_ang", [P, NT, HALF])
        turns = k.sb(ctx, "ro_turns", [P, NT, 2, HALF])
        with k.nc.Block() as block:

            @block.sync
            def _(sp):
                sp.dma_start(pos[:], k.dram["positions"]).then_inc(loaded.sem, 16)

            @block.vector
            def _(dve):
                def link(ins):
                    k.dve_chain.link(dve, ins)
                dve.wait_ge(loaded.sem, 16)
                link(dve.tensor_copy(posf[:], pos[:]))
                for a in range(NT):
                    link(dve.tensor_scalar(ang[:, a], k.row("freq"), posf[:, a:a + 1], None, ALU.mult))
                for s in range(2):
                    t = turns[:, :, s]
                    link(dve.tensor_scalar(t, ang[:], 1.0 / (2 * math.pi), 0.25 * s, ALU.mult, ALU.add))
                    link(dve.tensor_scalar(t, t, magic, None, ALU.add))
                    link(dve.tensor_scalar(t, t, magic, None, ALU.subtract))
                    r = cs[:, :, s]
                    link(dve.scalar_tensor_tensor(out=r, in0=t, scalar=-c1, in1=ang[:], op0=ALU.mult, op1=ALU.add))
                    link(dve.scalar_tensor_tensor(out=r, in0=t, scalar=-c2, in1=r, op0=ALU.mult, op1=ALU.add))
                    link(dve.scalar_tensor_tensor(out=r, in0=t, scalar=-c3, in1=r, op0=ALU.mult, op1=ALU.add))
                    if s:
                        link(dve.tensor_scalar(r, r, math.pi / 2, None, ALU.add))
                    link(dve.tensor_scalar(r, r, 3.1415925, -3.1415925, ALU.min, ALU.max))
                dve.sem_inc(reduced.sem, 1)

            @block.scalar
            def _(act):
                act.wait_ge(reduced.sem, 1)
                act.activation(cs[:], cs[:], ACT.Sin).then_inc(done.sem, 1)
                act.wait_ge(done.sem, 1)


def mla(k):
    norm_split(k, "attn0")
    with ExitStack() as ctx:
        cs = k.sb(ctx, "ml_cs", [P, NT, 2, HALF])
        angles(k, cs)
        v = k.sb(ctx, "ml_v", [P, NT, H_MLA, NOPE + DV])
        qt = k.sb(ctx, "ml_qt", [QK, H_MLA, T])
        kt = k.sb(ctx, "ml_kt", [QK, H_MLA, T])
        with ExitStack() as inner:
            down = k.sb(inner, "ml_down", [P, NT, W_DOWN])
            q = k.sb(inner, "ml_q", [P, NT, H_MLA, QK])
            kk = k.sb(inner, "ml_k", [P, NT, H_MLA, QK])
            gemm(k, k.xh, k.xl, KD, k.dram["mla_w_down"], W_DOWN, W_DOWN // 2, down)
            with ExitStack() as lat:
                y = k.sb(lat, "ml_y", [P, NT, R_Q + R_KV])
                s = k.sb(lat, "ml_s", [P, 2, NT])
                c_q, c_kv = slice(0, R_Q), slice(R_Q, R_Q + R_KV)
                norm_groups(k, [(down[:, :, c], y[:, :, c], None, y[:, :, c], s[:, n])
                                for n, c in enumerate((c_q, c_kv))], "lat")
                transposes(k, "lat", split_jobs(k, y[:, :, c_q], R_Q // P, k.xh, k.xl, k.col("q_lat"))
                           + split_jobs(k, y[:, :, c_kv], R_KV // P, k.xh[:, 4:], k.xl[:, 4:], k.col("kv_lat")))
            gemm(k, k.xh, k.xl, R_Q // P, k.dram["mla_w_uq"], H_MLA * QK, 512,
                 q[:].rearrange("p a h d -> p a (h d)"))
            gemm(k, k.xh[:, 4:], k.xl[:, 4:], R_KV // P, k.dram["mla_w_ukv"], H_MLA * (NOPE + DV), 512,
                 v[:].rearrange("p a h d -> p a (h d)"))
            head_norm_rope(k, down, v, q, kk, cs)
            jobs = []
            for dst, src in ((qt, q), (kt, kk)):
                for h in range(0, H_MLA, 2):
                    blocks = [(src[:, a, h + i], QK, i * T + a * P) for i in range(2) for a in range(NT)]
                    o = dst[:, h:h + 2].rearrange("p h t -> p (h t)")
                    if h % 4:
                        jobs.append((blocks, None, lambda dve, b, o=o: dve.tensor_copy(o, b[0:QK, :])))
                    else:
                        jobs.append((blocks, lambda act, b, o=o: act.activation(o, b[0:QK, :], ACT.Copy), None))
            transposes(k, "qk", jobs)
        causal = k.sb(ctx, "ml_causal", [P, NT, T])
        load(k, causal[:], k.dram["causal"])
        attention(k, H_MLA, lambda h: qt[:, h], lambda h: kt[:, h], lambda h, b: v[:, b, h, NOPE:], lambda h: causal[:],
                  QK ** -0.5, k.xh, k.xl)
    gemm(k, k.xh, k.xl, KD, k.dram["mla_w_o"], D, 512, k.h, add=True)


def load(k, dst, src):
    loaded = k.sig("ld_loaded")
    with k.nc.Block() as block:

        @block.sync
        def _(sp):
            sp.dma_start(dst, src).then_inc(loaded.sem, 16)
            sp.wait_ge(loaded.sem, loaded.at(16))

    loaded.advance(16)


def head_norm_rope(k, down, kv, q, kk, cs):
    copied = k.sig("hr_copied")
    with k.nc.Block() as block:

        @block.vector
        def _(dve):
            k.dve_chain.link(dve, dve.tensor_copy(kk[:, :, :, 0:NOPE].rearrange("p a h d -> p (a h) d"),
                                                  kv[:, :, :, 0:NOPE].rearrange("p a h d -> p (a h) d")))

        @block.scalar
        def _(act):
            for a in range(NT):
                k.act_chain.link(act, act.activation(
                    kk[:, a, :, NOPE:QK],
                    down[:, a, R_Q + R_KV:W_DOWN].unsqueeze(1).broadcast_to([P, H_MLA, ROPE]), ACT.Copy))

    with ExitStack() as ctx:
        work = k.sb(ctx, "hr_work", [P, NT * H_MLA, QK])
        s = k.sb(ctx, "hr_s", [P, 2, NT * H_MLA])
        for n, (x, gain) in enumerate(((q, "qn"), (kk, "kn"))):
            flat = x[:].rearrange("p a h d -> p (a h) d")
            norm_groups(k, [(flat, flat, k.row(gain), work[:], s[:, n])], gain)
        t = k.sb(ctx, "hr_t", [P, 4, H_MLA, HALF])
        with k.nc.Block() as block:

            @block.vector
            def _(dve):
                for x in (q, kk):
                    for a in range(NT):
                        x1, x2 = x[:, a, :, NOPE:NOPE + HALF], x[:, a, :, NOPE + HALF:QK]
                        sin, cos = (cs[:, a, s].unsqueeze(1).broadcast_to([P, H_MLA, HALF]) for s in range(2))
                        for n, (f, g) in enumerate(((x1, cos), (x2, sin), (x2, cos), (x1, sin))):
                            k.dve_chain.link(dve, dve.tensor_tensor(t[:, n], f, g, ALU.mult))
                        k.dve_chain.link(dve, dve.tensor_tensor(x1, t[:, 0], t[:, 1], ALU.subtract))
                        k.dve_chain.link(dve, dve.tensor_tensor(x2, t[:, 2], t[:, 3], ALU.add))



def product_keys(k, l, slots_i, slots_j, slots_g):
    G = NT * H_P
    norm_split(k, f"ffn{l}")
    with ExitStack() as ctx:
        s = k.sb(ctx, "pk_s", [P, NT, H_P, 2, NK])
        with ExitStack() as inner:
            q = k.sb(inner, "pk_q", [P, NT, D])
            qt = k.sb(inner, "pk_qt", [P, H_P, T])
            keys = k.sb(inner, "pk_keys", [P, 2, NK])
            gemm(k, k.xh, k.xl, KD, k.dram[f"w_query{l}"], D, 512, q)
            jobs = []
            for h in range(0, H_P, 2):
                blocks = [(q[:, a, (h + i) * P:(h + i + 1) * P], P, i * T + a * P) for i in range(2) for a in range(NT)]
                o = qt[:, h:h + 2].rearrange("p h t -> p (h t)")
                jobs.append((blocks, None, lambda dve, b, o=o: dve.tensor_copy(o, b[:])) if h % 4 else
                            (blocks, lambda act, b, o=o: act.activation(o, b[:], ACT.Copy), None))
            transposes(k, "pq", jobs)
            zeroed, loaded, scored = k.sig("pk_zeroed"), k.sig("pk_loaded"), k.sig("pk_scored")
            with k.nc.Block() as block:

                @block.gpsimd
                def _(pool):
                    pool.memset(keys[:], 0.0).then_inc(zeroed.sem, 1)

                @block.sync
                def _(sp):
                    sp.wait_ge(zeroed.sem, zeroed.at(1))
                    for c in range(2):
                        sp.dma_start(keys[c * 64:(c + 1) * 64, c, :], k.dram["sub_keys"][l, :, c, :])\
                          .then_inc(loaded.sem, 16)

                @block.tensor
                def _(pe):
                    pe.wait_ge(loaded.sem, loaded.at(32))
                    for h in range(H_P):
                        for a in range(NT):
                            last = pe.matmul(k.bank[h][:, a * T:(a + 1) * T], qt[:, h, a * P:(a + 1) * P],
                                             keys[:].rearrange("p c n -> p (c n)"), start=True, stop=True)
                        last.then_inc(scored.sem, 1)

                def banks(eng, copy, first, chain):
                    for h in range(first, H_P, 2):
                        eng.wait_ge(scored.sem, scored.at(h + 1))
                        chain.link(eng, copy(s[:, :, h].rearrange("p a c n -> p a (c n)"),
                                             k.bank[h][:].rearrange("p (a n) -> p a n", a=NT)))

                @block.scalar
                def _(act):
                    banks(act, lambda o, i: act.activation(o, i, ACT.Copy), 0, k.act_chain)

                @block.vector
                def _(dve):
                    banks(dve, dve.tensor_copy, 1, k.dve_chain)

            zeroed.advance(1)
            loaded.advance(32)
            scored.advance(H_P)

        top = k.sb(ctx, "pk_top", [P, G, 2, TOPK])
        at = k.sb(ctx, "pk_at", [P, G, 2, TOPK], U32)
        atf = k.sb(ctx, "pk_atf", [P, G, 2, TOPK])
        cand = k.sb(ctx, "pk_cand", [P, G, TOPK, TOPK])
        best = k.sb(ctx, "pk_best", [P, G, TOPK])
        pos = k.sb(ctx, "pk_pos", [P, G, TOPK], U32)
        half = k.sb(ctx, "pk_half", [P, 2, G, TOPK], U32)
        halff = k.sb(ctx, "pk_halff", [P, 2, G, TOPK])
        hot = k.sb(ctx, "pk_hot", [P, G, TOPK, TOPK])
        expert = k.sb(ctx, "pk_expert", [P, 2, G, TOPK])
        gate = k.sb(ctx, "pk_gate", [P, G, TOPK])
        total = k.sb(ctx, "pk_total", [P, G])
        count = k.sb(ctx, "pk_count", [P, TOPK], I32)
        countf = k.sb(ctx, "pk_countf", [P, TOPK])
        counted, raised, powered = k.sig("pk_counted"), k.sig("pk_raised"), k.sig("pk_powered")
        with k.nc.Block() as block:

            @block.gpsimd
            def _(pool):
                pool.iota(count[:], [[1, TOPK]], base=0, channel_multiplier=0).then_inc(counted.sem, 1)

            @block.vector
            def _(dve):
                def ordered(steps):
                    for ins in steps:
                        last = ins
                    k.dve_chain.link(dve, last)

                def top16(rows):
                    ordered(dve.max(m[:, 0:8], v) for v, m, _ in rows)
                    ordered(dve.max_index(i[:, 0:8], m[:, 0:8], v) for v, m, i in rows)
                    ordered(dve.match_replace(v, m[:, 0:8], v, -3.0e38) for v, m, _ in rows)
                    ordered(dve.max(m[:, 8:16], v) for v, m, _ in rows)
                    ordered(dve.max_index(i[:, 8:16], m[:, 8:16], v) for v, m, i in rows)

                top16([(s[:, g // H_P, g % H_P, c], top[:, g, c], at[:, g, c]) for g in range(G) for c in range(2)])
                dve.wait_ge(counted.sem, counted.at(1))
                ordered([dve.tensor_copy(countf[:], count[:]), dve.tensor_copy(atf[:], at[:]),
                         dve.tensor_tensor(cand[:], top[:, :, 0].unsqueeze(3).broadcast_to([P, G, TOPK, TOPK]),
                                           top[:, :, 1].unsqueeze(2).broadcast_to([P, G, TOPK, TOPK]), ALU.add)])
                top16([(cand[:, g].rearrange("p a b -> p (a b)"), best[:, g], pos[:, g]) for g in range(G)])
                ordered([dve.tensor_scalar(half[:, 0], pos[:], 4, None, ALU.logical_shift_right),
                         dve.tensor_scalar(half[:, 1], pos[:], 15, None, ALU.bitwise_and)])
                dve.tensor_tensor(gate[:], best[:], best[:, :, 0:1].broadcast_to([P, G, TOPK]), ALU.subtract)\
                   .then_inc(raised.sem, 1)
                ordered([dve.tensor_copy(halff[:], half[:])])
                for c in range(2):
                    wide = [P, G, TOPK, TOPK]
                    ordered([dve.tensor_tensor(hot[:], halff[:, c].unsqueeze(3).broadcast_to(wide),
                                               countf[:].unsqueeze(1).unsqueeze(1).broadcast_to(wide), ALU.is_equal)])
                    ordered([dve.tensor_tensor(hot[:], hot[:], atf[:, :, c].unsqueeze(2).broadcast_to(wide),
                                               ALU.mult)])
                    ordered([dve.tensor_reduce(expert[:, c], hot[:], AX_X, ALU.add)])
                dve.wait_ge(powered.sem, powered.at(1))
                ordered([dve.tensor_reduce(total[:], gate[:], AX_X, ALU.add)])
                ordered([dve.reciprocal(total[:], total[:])])
                ordered([dve.tensor_tensor(gate[:], gate[:], total[:].unsqueeze(2).broadcast_to([P, G, TOPK]),
                                           ALU.mult)])

            @block.scalar
            def _(act):
                act.wait_ge(raised.sem, raised.at(1))
                act.activation(gate[:], gate[:], ACT.Exp).then_inc(powered.sem, 1)

        for x in (counted, raised, powered):
            x.advance(1)
        jobs = []
        for dst, src in ((slots_i, expert[:, 0]), (slots_j, expert[:, 1]), (slots_g, gate[:])):
            flat = src.rearrange("p g s -> p (g s)")
            jobs.append(([(flat[:, a * SLOTS:(a + 1) * SLOTS], P, a * P) for a in range(NT)], None,
                         lambda dve, b, o=dst: dve.tensor_copy(o[:], b[:, 0:T])))
        transposes(k, "slots", jobs)


def scatter_gates(k, slots_i, slots_j, slots_g, g):
    hot_j, hot_i, summed, stored = k.sig("sc_hot_j"), k.sig("sc_hot_i"), k.sig("sc_summed"), k.sig("sc_stored")
    counted = k.sig("sc_counted")
    N = 4
    groups = T // N
    with ExitStack() as ctx:
        count = k.sb(ctx, "sc_count", [P, NK], I32)
        countf = k.sb(ctx, "sc_countf", [P, NK])
        a = k.sb(ctx, "sc_a", [P, 2, N, NK])
        b = k.sb(ctx, "sc_b", [P, 2, N, NK])

        def looped(eng, body):
            body(0, 0)
            body(1, 1)
            with eng.Fori(1, groups // 2) as m:
                body(2 * m, 0)
                body(2 * m + 1, 1)

        with k.nc.Block() as block:

            @block.gpsimd
            def _(pool):
                k.pool_chain.link(pool, pool.iota(count[:], [[1, NK]], base=0, channel_multiplier=0))
                pool.tensor_copy(countf[:], count[:]).then_inc(counted.sem, 1)

            @block.vector
            def _(dve):
                dve.wait_ge(counted.sem, counted.at(1))

                def body(n, r):
                    if not (isinstance(n, int) and n < 2):
                        dve.wait_ge(summed.sem, summed.at(n - 1))
                    dve.tensor_tensor(a[:, r], countf[:].unsqueeze(1).broadcast_to([P, N, NK]),
                                      slots_j[:, bass.ds(n * N, N)].unsqueeze(2).broadcast_to([P, N, NK]),
                                      ALU.is_equal).then_inc(hot_j.sem, 1)
                    for t in range(N):
                        last = dve.tensor_scalar(b[:, r, t], countf[:], slots_i[:, bass.ds(n * N + t, 1)],
                                                 slots_g[:, bass.ds(n * N + t, 1)], ALU.is_equal, ALU.mult)
                    last.then_inc(hot_i.sem, 1)
                looped(dve, body)

            @block.tensor
            def _(pe):
                def body(n, r):
                    pe.wait_ge(hot_j.sem, hot_j.at(n + 1))
                    pe.wait_ge(hot_i.sem, hot_i.at(n + 1))
                    if not (isinstance(n, int) and n < 2):
                        pe.wait_ge(stored.sem, stored.at(n - 1))
                    for t in range(N):
                        last = pe.matmul(k.bank[r][:, t * NK:(t + 1) * NK], a[:, r, t], b[:, r, t],
                                         start=True, stop=True)
                    last.then_inc(summed.sem, 1)
                looped(pe, body)

            @block.scalar
            def _(act):
                def body(n, r):
                    act.wait_ge(summed.sem, summed.at(n + 1))
                    act.activation(g[:, :, bass.ds(n * N, N)], k.bank[r][:].rearrange("p (t i) -> p i t", t=N),
                                   ACT.Copy).then_inc(stored.sem, 1)
                looped(act, body)

    counted.advance(1)
    for x in (hot_j, hot_i, summed, stored):
        x.advance(groups)


def two_products(k, name, n, na, a_dram, b_dram, gates=None):
    s = {x: k.sig(f"{name}_{x}") for x in ("a_hi", "a_lo", "b_hi", "b_lo", "first", "bent", "middle", "m_hi",
                                           "m_lo", "second")}
    a_in = [k.sig(f"{name}_a_in{r}") for r in range(2)]
    b_in = [k.sig(f"{name}_b_in{r}") for r in range(2)]
    with ExitStack() as ctx:
        a_raw = k.sb(ctx, f"{name}_a_raw", [P, 2, na, D])
        b_raw = k.sb(ctx, f"{name}_b_raw", [P, 2, D])
        ah = k.sb(ctx, f"{name}_ah", [P, 2, na, KD, P], F32R)
        al = k.sb(ctx, f"{name}_al", [P, 2, na, KD, P], F32R)
        bh = k.sb(ctx, f"{name}_bh", [P, 2, D], F32R)
        bl = k.sb(ctx, f"{name}_bl", [P, 2, D], F32R)
        bent = k.sb(ctx, f"{name}_bent", [P, 2, T])
        mid = k.sb(ctx, f"{name}_mid", [P, 2, T])
        mh = k.sb(ctx, f"{name}_mh", [P, 2, T], F32R)
        ml = k.sb(ctx, f"{name}_ml", [P, 2, T], F32R)

        def first_ps(r, x):
            return k.bank[r][:, x * T:(x + 1) * T]

        def second_ps(a, c):
            return k.bank[4 + 2 * a + c][:]

        def stepped(eng, step):
            def fixed(i):
                step(i, i % 2, i < n, i >= 2, i + 1 < n)
            for i in range(4):
                fixed(i)
            if n > 8:
                with eng.Fori(0, (n - 6) // 2) as m:
                    step(2 * m + 4, 0, True, True, True)
                    step(2 * m + 5, 1, True, True, True)
            for i in range(n - 2 if n > 8 else 4, n + 2):
                fixed(i)

        def past(i, least):
            return not (isinstance(i, int) and i < least)

        with k.nc.Block() as block:

            @block.sync
            def _(sp):
                def load_a(i, r):
                    if past(i, 2):
                        sp.wait_ge(s["a_lo"].sem, s["a_lo"].at(i - 1))
                    sp.dma_start(a_raw[:, r], a_dram(i)).then_inc(a_in[r].sem, 16)

                def step(i, r, first, second, ahead):
                    if ahead:
                        load_a(i + 1, 1 - r)
                    if past(i, 1) and (not isinstance(i, int) or i <= n):
                        if past(i, 3):
                            sp.wait_ge(s["b_lo"].sem, s["b_lo"].at(i - 2))
                        sp.dma_start(b_raw[:, 1 - r], b_dram(i - 1)).then_inc(b_in[1 - r].sem, 16)

                load_a(0, 0)
                stepped(sp, step)

            def landed(eng, sems, i, r):
                eng.wait_ge(sems[r].sem, sems[r].at((i - r) * 8 + 16))

            @block.scalar
            def _(act):
                def split_a(i, r):
                    landed(act, a_in, i, r)
                    if past(i, 2):
                        act.wait_ge(s["first"].sem, s["first"].at(i - 1))
                    act.activation(ah[:, r].rearrange("p x k e -> p (x k e)"),
                                   a_raw[:, r].rearrange("p x n -> p (x n)"), ACT.Copy).then_inc(s["a_hi"].sem, 1)

                def step(i, r, first, second, ahead):
                    if ahead:
                        split_a(i + 1, 1 - r)
                    if first:
                        act.wait_ge(s["first"].sem, s["first"].at(i + 1))
                        if past(i, 2):
                            act.wait_ge(s["middle"].sem, s["middle"].at(i - 1))
                        if na == 1:
                            act.activation(bent[:, r], first_ps(r, 0), ACT.Gelu).then_inc(s["bent"].sem, 1)
                        else:
                            act.activation(bent[:, r], first_ps(r, 0), ACT.Exp, scale=-1.0).then_inc(s["bent"].sem, 1)
                    if past(i, 1) and (not isinstance(i, int) or i <= n):
                        landed(act, b_in, i - 1, 1 - r)
                        if past(i, 3):
                            act.wait_ge(s["second"].sem, s["second"].at(i - 2))
                        act.activation(bh[:, 1 - r], b_raw[:, 1 - r], ACT.Copy).then_inc(s["b_hi"].sem, 1)
                    if first:
                        act.wait_ge(s["middle"].sem, s["middle"].at(i + 1))
                        if past(i, 2):
                            act.wait_ge(s["second"].sem, s["second"].at(i - 1))
                        act.activation(mh[:, r], mid[:, r], ACT.Copy).then_inc(s["m_hi"].sem, 1)

                split_a(0, 0)
                stepped(act, step)

            @block.vector
            def _(dve):
                links = k.dve_chain
                LINKS = 3

                def split_a(i, r):
                    dve.wait_ge(s["a_hi"].sem, s["a_hi"].at(i + 1))
                    dve.tensor_tensor(al[:, r].rearrange("p x k e -> p (x k e)"),
                                      a_raw[:, r].rearrange("p x n -> p (x n)"),
                                      ah[:, r].bitcast(F32).rearrange("p x k e -> p (x k e)"), ALU.subtract)\
                       .then_inc(s["a_lo"].sem, 1)

                def step(i, r, first, second, ahead):
                    if ahead:
                        split_a(i + 1, 1 - r)
                    if first:
                        dve.wait_ge(s["bent"].sem, s["bent"].at(i + 1))
                        if past(i, 2):
                            dve.wait_ge(s["m_lo"].sem, s["m_lo"].at(i - 1))
                        if na == 1:
                            dve.tensor_tensor(mid[:, r], bent[:, r], gates[:, i, :], ALU.mult)\
                               .then_inc(s["middle"].sem, 1)
                        else:
                            chain = [
                                lambda: dve.tensor_scalar(bent[:, r], bent[:, r], 1.0, None, ALU.add),
                                lambda: dve.reciprocal(bent[:, r], bent[:, r]),
                                lambda: dve.tensor_tensor(mid[:, r], first_ps(r, 0), bent[:, r], ALU.mult),
                            ]
                            for c, make in enumerate(chain):
                                make().then_inc(links.sem, 1)
                                dve.wait_ge(links.sem, LINKS * i + c + 1 + links.count)
                            dve.tensor_tensor(mid[:, r], mid[:, r], first_ps(r, 1), ALU.mult)\
                               .then_inc(s["middle"].sem, 1)
                    if past(i, 1) and (not isinstance(i, int) or i <= n):
                        dve.wait_ge(s["b_hi"].sem, s["b_hi"].at(i))
                        dve.tensor_tensor(bl[:, 1 - r], b_raw[:, 1 - r], bh[:, 1 - r].bitcast(F32), ALU.subtract)\
                           .then_inc(s["b_lo"].sem, 1)
                    if first:
                        dve.wait_ge(s["m_hi"].sem, s["m_hi"].at(i + 1))
                        dve.tensor_tensor(ml[:, r], mid[:, r], mh[:, r].bitcast(F32), ALU.subtract)\
                           .then_inc(s["m_lo"].sem, 1)

                split_a(0, 0)
                stepped(dve, step)
                if na == 2:
                    links.count += LINKS * n
                dve.wait_ge(s["second"].sem, s["second"].at(n))
                for a in range(NT):
                    for c in range(2):
                        o = k.h[:, a, c * 512:(c + 1) * 512]
                        links.link(dve, dve.tensor_tensor(o, o, second_ps(a, c), ALU.add))

            @block.tensor
            def _(pe):
                def step(i, r, first, second, ahead):
                    if first:
                        pe.wait_ge(s["a_hi"].sem, s["a_hi"].at(i + 1))
                        pe.wait_ge(s["a_lo"].sem, s["a_lo"].at(i + 1))
                        if past(i, 2):
                            pe.wait_ge(s["middle"].sem, s["middle"].at(i - 1))
                        for x in range(na):
                            for c in range(KD):
                                pe.matmul(first_ps(r, x), ah[:, r, x, c], k.xh[:, c], start=(c == 0), stop=False)
                                pe.matmul(first_ps(r, x), ah[:, r, x, c], k.xl[:, c], start=False, stop=False)
                                last = pe.matmul(first_ps(r, x), al[:, r, x, c], k.xh[:, c], start=False,
                                                 stop=(c == KD - 1))
                        last.then_inc(s["first"].sem, 1)
                    if second:
                        for x in ("b_hi", "b_lo", "m_hi", "m_lo"):
                            pe.wait_ge(s[x].sem, s[x].at(i - 1))
                        start = isinstance(i, int) and i == 2
                        stop = isinstance(i, int) and i == n + 1
                        for a in range(NT):
                            t = slice(a * P, (a + 1) * P)
                            for x, (m, b) in enumerate(((mh, bh), (mh, bl), (ml, bh))):
                                for c in range(2):
                                    last = pe.matmul(second_ps(a, c), m[:, r, t], b[:, r, c * 512:(c + 1) * 512],
                                                     start=(start and x == 0), stop=(stop and x == 2),
                                                     skip_group_check=True)
                        last.then_inc(s["second"].sem, 1)
                stepped(pe, step)

    for x in s.values():
        x.advance(n)
    for r in range(2):
        a_in[r].advance(8 * n)
        b_in[r].advance(8 * n)


def peer(k, l):
    with ExitStack() as ctx:
        i, j, gate = (k.sb(ctx, f"pe_slots_{x}", [P, T]) for x in "ijg")
        product_keys(k, l, i, j, gate)
        g = k.sb(ctx, "pe_g", [P, NK, T])
        scatter_gates(k, i, j, gate, g)
        u, v = k.dram["peer_u"], k.dram["peer_v"]
        two_products(k, "ex", NK, 1, lambda t: u[l, bass.ds(t, 1)].rearrange("o p k e -> p o (k e)"),
                     lambda t: v[l, bass.ds(t, 1)].rearrange("o p d -> p (o d)"), g)


def gla(k):
    norm_split(k, "attn1")
    with ExitStack() as ctx:
        proj = k.sb(ctx, "gl_proj", [P, NT, W_GLA])
        gemm(k, k.xh, k.xl, KD, k.dram["gla_w_in"], G_LOW, 512, proj)
        narrow_gemm(k, k.dram["gla_w_in"], G_LOW, R_G, proj)
        o = k.sb(ctx, "gl_o", [P, NT, H_G, DV_G])
        with ExitStack() as inner:
            gla_core(k, inner, proj, o)
        gated_output(k, proj, o)
        transposes(k, "go", split_jobs(k, o[:].rearrange("p a h d -> p a (h d)"), KD, k.xh, k.xl, k.col("one")))
    gemm(k, k.xh, k.xl, KD, k.dram["gla_w_o"], D, 512, k.h, add=True)


def gla_core(k, ctx, proj, o):
    N = H_G * NT
    qt = k.sb(ctx, "gl_qt", [P, H_G, T])
    kt = k.sb(ctx, "gl_kt", [P, H_G, T])
    low = k.sb(ctx, "gl_low", [R_G, T])
    jobs = []
    for dst, c0 in ((qt, G_Q), (kt, G_K)):
        for h in range(0, H_G, 2):
            blocks = [(proj[:, a, c0 + (h + i) * DK_G:c0 + (h + i + 1) * DK_G], P, i * T + a * P)
                      for i in range(2) for a in range(NT)]
            d = dst[:, h:h + 2].rearrange("p h t -> p (h t)")
            jobs.append((blocks, None, lambda dve, b, d=d: dve.tensor_copy(d, b[:])) if h % 4 else
                        (blocks, lambda act, b, d=d: act.activation(d, b[:], ACT.Copy), None))
    jobs.append(([(proj[:, a, G_LOW:W_GLA], R_G, a * P) for a in range(NT)], None,
                 lambda dve, b: dve.tensor_copy(low[:], b[0:R_G, 0:T])))
    transposes(k, "gl", jobs)

    w2 = k.sb(ctx, "gl_w2", [R_G, H_G * DK_G])
    z = k.sb(ctx, "gl_z", [P, H_G, T])
    e = k.sb(ctx, "gl_e", [P, H_G, T])
    fresh = k.sb(ctx, "gl_fresh", [P, H_G, NCH, CH])
    b = k.sb(ctx, "gl_b", [P, H_G, NCH, CH])
    left = k.sb(ctx, "gl_left", [P, H_G, NCH, CH])
    qd = k.sb(ctx, "gl_qd", [P, H_G, T])
    ki = k.sb(ctx, "gl_ki", [P, H_G, T])
    kd = k.sb(ctx, "gl_kd", [P, H_G, T])
    decay = k.sb(ctx, "gl_decay", [P, H_G, NCH])
    load(k, w2[:], k.dram["gla_w_g2"])
    made, folded, logged, summed, powered = (k.sig(f"gl_{x}") for x in ("made", "folded", "logged", "summed",
                                                                       "powered"))
    masked = k.sig("gl_masked")
    with k.nc.Block() as block:

        @block.tensor
        def _(pe):
            for h in range(H_G):
                pe.matmul(k.bank[h][:, 0:T], w2[:, h * DK_G:(h + 1) * DK_G], low[:], start=True, stop=True)\
                  .then_inc(made.sem, 1)

        @block.gpsimd
        def _(pool):
            k.pool_chain.link(pool, pool.memset(fresh[:], 1.0))
            k.pool_chain.link(pool, pool.memset(fresh[:, :, :, 0:1], 0.0))
            pool.nop().then_inc(masked.sem, 1)

        @block.vector
        def _(dve):
            def link(ins):
                k.dve_chain.link(dve, ins)
            dve.wait_ge(made.sem, made.at(H_G))
            for h in range(H_G):
                ins = dve.tensor_scalar(z[:, h], k.bank[h][:, 0:T], k.col("b_g")[:, h:h + 1], None, ALU.add)
            link(ins)
            dve.scalar_tensor_tensor(out=e[:], in0=z[:], scalar=-1.0, in1=z[:], op0=ALU.mult, op1=ALU.min)\
               .then_inc(folded.sem, 1)
            link(dve.tensor_scalar(z[:], z[:], 0.0, None, ALU.min))
            dve.wait_ge(logged.sem, logged.at(1))
            link(dve.tensor_tensor(z[:], z[:], e[:], ALU.subtract))
            link(dve.tensor_scalar(z[:], z[:], 1.0 / TAU, None, ALU.mult))
            dve.wait_ge(masked.sem, masked.at(1))
            link(dve.tensor_tensor_scan(b[:].rearrange("p h n c -> p (h n c)"),
                                        fresh[:].rearrange("p h n c -> p (h n c)"),
                                        z[:].rearrange("p h t -> p (h t)"), 0.0, ALU.mult, ALU.add))
            dve.tensor_tensor(left[:], b[:, :, :, CH - 1:CH].broadcast_to([P, H_G, NCH, CH]), b[:], ALU.subtract)\
               .then_inc(summed.sem, 1)
            flat = [x[:].rearrange("p h t -> p (h t)") for x in (qt, kt, qd, ki, kd)]
            dve.wait_ge(powered.sem, powered.at(1))
            dve.scalar_tensor_tensor(out=flat[2], in0=flat[0], scalar=DK_G ** -0.5,
                                     in1=qd[:].rearrange("p h t -> p (h t)"), op0=ALU.mult, op1=ALU.mult)
            dve.wait_ge(powered.sem, powered.at(2))
            dve.tensor_tensor(flat[3], flat[1], flat[3], ALU.mult)
            dve.wait_ge(powered.sem, powered.at(3))
            link(dve.tensor_tensor(flat[4], flat[1], flat[4], ALU.mult))

        @block.scalar
        def _(act):
            act.wait_ge(folded.sem, folded.at(1))
            k.act_chain.link(act, act.activation(e[:], e[:], ACT.Exp))
            act.activation(e[:], e[:], ACT.Ln, bias=k.col("one")[:, 0:1]).then_inc(logged.sem, 1)
            act.wait_ge(summed.sem, summed.at(1))
            act.activation(qd[:], b[:].rearrange("p h n c -> p h (n c)"), ACT.Exp).then_inc(powered.sem, 1)
            act.activation(ki[:], b[:].rearrange("p h n c -> p h (n c)"), ACT.Exp, scale=-1.0).then_inc(powered.sem, 1)
            act.activation(kd[:], left[:].rearrange("p h n c -> p h (n c)"), ACT.Exp).then_inc(powered.sem, 1)
            k.act_chain.link(act, act.activation(decay[:], b[:, :, :, CH - 1], ACT.Exp))

    made.advance(H_G)
    powered.advance(3)
    for s in (folded, logged, summed, masked):
        s.advance(1)

    at = k.sb(ctx, "gl_at", [P, N, CH])
    kdn = k.sb(ctx, "gl_kdn", [P, N, DK_G])
    state = k.sb(ctx, "gl_state", [P, NCH - 1, H_G, DV_G])
    weighed, copied, selected = k.sig("gl_weighed"), k.sig("gl_copied"), k.sig("gl_selected")
    turned, keyed, added, carried = k.sig("gl_turned"), k.sig("gl_keyed"), k.sig("gl_added"), k.sig("gl_carried")
    mixed = k.sig("gl_mixed")

    def rows(n):
        return slice(CH * (n % 2), CH * (n % 2) + CH)

    def values(n, h):
        return proj[rows(n), n // 2, G_V + h * DV_G:G_V + (h + 1) * DV_G]

    with k.nc.Block() as block:

        @block.tensor
        def _(pe):
            for h in range(H_G):
                for n in range(NCH):
                    t = slice(n * CH, (n + 1) * CH)
                    g = h * NT + n // 2
                    last = pe.matmul(k.bank[0][rows(n), g * CH:(g + 1) * CH], ki[:, h, t], qd[:, h, t], start=True,
                                     stop=True, skip_group_check=True)
            last.then_inc(weighed.sem, 1)
            for h in range(H_G):
                for a in range(NT):
                    last = pe.transpose(k.bank[1 + h // 2][:, (h % 2 * NT + a) * P:(h % 2 * NT + a + 1) * P],
                                        kd[:, h, a * P:(a + 1) * P], k.ident[:])
            last.then_inc(turned.sem, 1)
            pe.wait_ge(keyed.sem, keyed.at(1))
            for n in range(NCH - 1):
                if n:
                    pe.wait_ge(carried.sem, carried.at(n))
                for h in range(H_G):
                    last = pe.matmul(k.bank[3 + h // 2][:, h % 2 * DV_G:(h % 2 + 1) * DV_G],
                                     kdn[rows(n), h * NT + n // 2], values(n, h), start=True, stop=True)
                last.then_inc(added.sem, 1)
            pe.wait_ge(selected.sem, selected.at(1))
            pe.wait_ge(carried.sem, carried.at(NCH - 1))
            for h in range(H_G):
                for a in range(NT):
                    g = h * NT + a
                    if g >= 3:
                        pe.wait_ge(mixed.sem, mixed.at(g - 2))
                    for n in (2 * a, 2 * a + 1):
                        ps = k.bank[5 + g % 3][rows(n), 0:DV_G]
                        last = pe.matmul(ps, at[rows(n), g], values(n, h), start=True, stop=(n == 0),
                                         skip_group_check=True)
                        if n:
                            last = pe.matmul(ps, qd[:, h, n * CH:(n + 1) * CH], state[:, n - 1, h], start=False,
                                             stop=True, skip_group_check=True)
                    last.then_inc(weighed.sem, 1)

        @block.scalar
        def _(act):
            act.wait_ge(weighed.sem, weighed.at(1))
            act.activation(at[:].rearrange("p g t -> p (g t)"), k.bank[0][:], ACT.Copy).then_inc(copied.sem, 1)
            act.wait_ge(turned.sem, turned.at(1))
            for i in range(2):
                last = act.activation(kdn[:, i * 4:(i + 1) * 4].rearrange("p g d -> p (g d)"), k.bank[1 + i][:],
                                      ACT.Copy)
            last.then_inc(keyed.sem, 1)
            for h in range(H_G):
                for a in range(NT):
                    g = h * NT + a
                    act.wait_ge(weighed.sem, weighed.at(g + 2))
                    act.activation(o[:, a, h], k.bank[5 + g % 3][:, 0:DV_G], ACT.Copy).then_inc(mixed.sem, 1)

        @block.gpsimd
        def _(pool):
            pool.wait_ge(copied.sem, copied.at(1))
            for r in range(2):
                part = at[r * CH:(r + 1) * CH]
                k.pool_chain.link(pool, pool.affine_select(out=part, in_=part, compare_op=ALU.is_ge, fill=0.0,
                                                           base=0, pattern=[[0, N], [1, CH]],
                                                           channel_multiplier=-1))
            pool.nop().then_inc(selected.sem, 1)

        @block.vector
        def _(dve):
            for n in range(NCH - 1):
                dve.wait_ge(added.sem, added.at(n + 1))
                for h in range(H_G):
                    ps = k.bank[3 + h // 2][:, h % 2 * DV_G:(h % 2 + 1) * DV_G]
                    if n == 0:
                        last = dve.tensor_copy(state[:, 0, h], ps)
                    else:
                        last = dve.scalar_tensor_tensor(out=state[:, n, h], in0=state[:, n - 1, h],
                                                        scalar=decay[:, h, n:n + 1], in1=ps, op0=ALU.mult,
                                                        op1=ALU.add)
                last.then_inc(carried.sem, 1)
                dve.wait_ge(carried.sem, carried.at(n + 1))

    weighed.advance(1 + N)
    mixed.advance(N)
    for s in (copied, selected, turned, keyed):
        s.advance(1)
    added.advance(NCH - 1)
    carried.advance(NCH - 1)


def sigmoid_steps(dve, k, x, e):
    k.dve_chain.link(dve, dve.tensor_scalar(e, e, 1.0, None, ALU.add))
    k.dve_chain.link(dve, dve.reciprocal(e, e))
    if x is not None:
        k.dve_chain.link(dve, dve.tensor_tensor(e, x, e, ALU.mult))


def gated_output(k, proj, o):
    with ExitStack() as ctx:
        e = k.sb(ctx, "go_e", [P, NT, D])
        work = k.sb(ctx, "go_work", [P, NT * H_G, DV_G])
        s = k.sb(ctx, "go_s", [P, NT * H_G])
        flat = o[:].rearrange("p a h d -> p (a h) d")
        norm_groups(k, [(flat, flat, k.row("on"), work[:], s[:])], "on")
        powered = k.sig("go_powered")
        r = proj[:, :, G_R:G_R + D]
        with k.nc.Block() as block:

            @block.scalar
            def _(act):
                act.activation(e[:], r, ACT.Exp, scale=-1.0).then_inc(powered.sem, 1)

            @block.vector
            def _(dve):
                dve.wait_ge(powered.sem, powered.at(1))
                sigmoid_steps(dve, k, r, e[:])
                flat_o = o[:].rearrange("p a h d -> p a (h d)")
                k.dve_chain.link(dve, dve.tensor_tensor(flat_o, flat_o, e[:], ALU.mult))

        powered.advance(1)


def second_block(k):
    norm_split(k, "mix2")
    with ExitStack() as ctx:
        proj = k.sb(ctx, "sb_proj", [P, NT, W_IN2])
        w = k.dram["w_in_2"]
        main = W_IN2 // 512 * 512
        gemm(k, k.xh, k.xl, KD, w[:, 0:main], main, 512, proj)
        gemm(k, k.xh, k.xl, KD, w[:, main:W_IN2], W_IN2 - main, W_IN2 - main, proj[:, :, main:W_IN2])
        ya = k.sb(ctx, "sb_ya", [P, NT, D])
        with ExitStack() as inner:
            yb = k.sb(inner, "sb_yb", [P, NT, D])
            bias = k.sb(inner, "sb_bias", [P, H_A, NT, T])
            qt = k.sb(inner, "sb_qt", [P, H_A // 2, T])
            kt = k.sb(inner, "sb_kt", [P, H_A // 2, T])
            qbt = k.sb(inner, "sb_qbt", [P, H_B // 2, T])
            kbt = k.sb(inner, "sb_kbt", [P, KV_B, T])
            with ExitStack() as norms:
                heads = k.sb(norms, "sb_heads", [P, NT * H_A, DH])
                s = k.sb(norms, "sb_s", [P, 4, NT * H_A])
                kb = k.sb(norms, "sb_kb", [P, NT, 2 * KV_B, DH])
                for n, (c0, gain) in enumerate(((A_Q, "qa"), (A_K, "ka"), (B_Q, "qb"))):
                    for a in range(NT):
                        x = proj[:, a, c0:c0 + H_A * DH].rearrange("p (h d) -> p h d", d=DH)
                        norm_groups(k, [(x, x, k.row(gain), heads[:, 0:H_A], s[:, n, a * H_A:(a + 1) * H_A])], gain)
                for a in range(NT):
                    x = proj[:, a, B_K:B_K + KV_B * DH].rearrange("p (h d) -> p h d", d=DH)
                    norm_groups(k, [(x, kb[:, a, 0:KV_B], k.row("kb"), heads[:, 0:KV_B],
                                     s[:, 3, a * KV_B:(a + 1) * KV_B])], "kb")
                swap(k, kb)
                turn_pairs(k, qt, proj[:, :, A_Q:A_Q + A_W])
                turn_pairs(k, kt, proj[:, :, A_K:A_K + A_W])
                turn_pairs(k, qbt, proj[:, :, B_Q:B_Q + A_W])
                turn_pairs(k, kbt, kb[:].rearrange("p a h d -> p a (h d)"))

            def half(h):
                return slice(DH * (h % 2), DH * (h % 2) + DH)

            load(k, bias[:], k.dram["bias_a"])
            attention(k, H_A, lambda h: qt[half(h), h // 2], lambda h: kt[half(h), h // 2],
                      lambda h, b: proj[:, b, A_V + h * DH:A_V + (h + 1) * DH], lambda h: bias[:, h], DH ** -0.5,
                      k.xh, k.xl)
            gemm(k, k.xh, k.xl, A_W // P, k.dram["w_branch_a"], D, 512, ya)
            load(k, bias[:], k.dram["bias_b"])

            def key_head(h):
                return h // (H_B // KV_B)

            attention(k, H_B, lambda h: qbt[half(h), h // 2], lambda h: kbt[half(h), (h % 2) ^ key_head(h)],
                      lambda h, b: proj[:, b, B_V + key_head(h) * DH:B_V + (key_head(h) + 1) * DH],
                      lambda h: bias[:, h], DH ** -0.5, k.xh, k.xl, sink=k.row("sink"))
            gemm(k, k.xh, k.xl, A_W // P, k.dram["w_branch_b"], D, 512, yb)
            mix_gates(k, proj, ya, yb)
        transposes(k, "y", split_jobs(k, ya, KD, k.xh, k.xl, k.col("one")))
    gemm(k, k.xh, k.xl, KD, k.dram["w_out"], D, 512, k.h, add=True)
    norm_split(k, "ffn2")
    up, down = k.dram["w_gate_up"], k.dram["w_down_2"]
    two_products(k, "ff", NFT, 2, lambda t: up[bass.ds(t, 1)].rearrange("o p x k e -> p (o x) (k e)"),
                 lambda t: down[bass.ds(t, 1)].rearrange("o p d -> p (o d)"))


def swap(k, kb):
    with k.nc.Block() as block:

        @block.vector
        def _(dve):
            for h in range(KV_B):
                k.dve_chain.link(dve, dve.tensor_copy(kb[:, :, KV_B + h], kb[:, :, KV_B - 1 - h]))


def turn_pairs(k, dst, src):
    jobs = []
    for c in range(0, dst.shape[1], 2):
        blocks = [(src[:, a, (c + i) * P:(c + i + 1) * P], P, i * T + a * P) for i in range(2) for a in range(NT)]
        d = dst[:, c:c + 2].rearrange("p c t -> p (c t)")
        jobs.append((blocks, None, lambda dve, b, d=d: dve.tensor_copy(d, b[:])) if c % 4 else
                    (blocks, lambda act, b, d=d: act.activation(d, b[:], ACT.Copy), None))
    transposes(k, "tp", jobs)


def mix_gates(k, proj, ya, yb):
    powered = k.sig("mg_powered")
    with ExitStack() as ctx:
        e = k.sb(ctx, "mg_e", [P, 2, NT, D])
        with k.nc.Block() as block:

            @block.scalar
            def _(act):
                for n, c0 in enumerate((GATE_A, GATE_B)):
                    act.activation(e[:, n], proj[:, :, c0:c0 + D], ACT.Exp, scale=-1.0).then_inc(powered.sem, 1)

            @block.vector
            def _(dve):
                for n, y in enumerate((ya, yb)):
                    dve.wait_ge(powered.sem, powered.at(n + 1))
                    sigmoid_steps(dve, k, y[:], e[:, n])
                k.dve_chain.link(dve, dve.tensor_tensor(ya[:], e[:, 0], e[:, 1], ALU.add))

    powered.advance(2)


def build_program(nc, dram, out):
    with ExitStack() as ctx:
        k = Kernel(nc, ctx, dram)
        setup(k)
        mla(k)
        peer(k, 0)
        gla(k)
        peer(k, 1)
        second_block(k)
        stored = k.sig("stored")
        with nc.Block() as block:

            @block.sync
            def _(sp):
                sp.dma_start(out.rearrange("b (a p) d -> p (b a) d", p=P), k.h[:]).then_inc(stored.sem, 16)
                sp.wait_ge(stored.sem, 16)


def t5_bucket(rel):
    half = 16
    max_exact = half // 2
    ret = (rel > 0).astype(np.int32) * half
    n = np.abs(rel)
    large = max_exact + (np.log(np.maximum(n, 1) / max_exact) / np.log(128 / max_exact)
                         * (half - max_exact)).astype(np.int32)
    large = np.minimum(large, half - 1)
    return ret + np.where(n < max_exact, n, large)


def layout(x, positions, attn_norm_g, ffn_norm_g, mla_w_down, mla_g_q_lat, mla_w_uq, mla_g_kv_lat, mla_w_ukv,
           mla_g_qn, mla_g_kn, mla_w_o, gla_w_in, gla_w_g2, gla_b_g, gla_g_on, gla_w_o, peer_w_query, peer_sub_keys,
           peer_u, peer_v, norm_mix_2, w_in_2, q_norm_a_2, k_norm_a_2, rpb_a_2, q_norm_b_2, k_norm_b_2, sink_b_2,
           t5_table_2, w_branch_a_2, w_branch_b_2, w_out_2, norm_ffn_2, w_gate_2, w_up_2, w_down_2):
    col = {
        "attn0": attn_norm_g[0], "attn1": attn_norm_g[1], "ffn0": ffn_norm_g[0], "ffn1": ffn_norm_g[1],
        "mix2": norm_mix_2[0], "ffn2": norm_ffn_2[0], "q_lat": mla_g_q_lat[0], "kv_lat": mla_g_kv_lat[0],
        "b_g": gla_b_g[0], "one": np.ones(D, np.float32), "eps": np.full(P, EPS, np.float32),
    }
    freq = np.float32(10000.0) ** (-np.arange(HALF, dtype=np.float32) / np.float32(HALF))
    row = {"qn": mla_g_qn[0], "kn": mla_g_kn[0], "on": gla_g_on[0], "qa": q_norm_a_2[0], "ka": k_norm_a_2[0],
           "qb": q_norm_b_2[0], "kb": k_norm_b_2[0], "sink": sink_b_2[0], "freq": freq}
    q, key = np.arange(T)[:, None], np.arange(T)[None, :]
    qr, qc, kr, kc = q // 64, q % 64, key // 64, key % 64
    start = np.clip(qc - 8, 0, 48)
    near = (kc >= start) & (kc < start + 16)
    bias_a = np.where(near[:, :, None], rpb_a_2[0][kr - qr + 7, np.clip(kc - qc, -15, 15) + 15], np.float32(NEG))
    rel = key - q
    bias_b = np.where((np.abs(rel) <= 128)[:, :, None], t5_table_2[t5_bucket(rel)], np.float32(NEG))
    causal = np.where(key <= q, np.float32(0), np.float32(NEG))
    tiles = lambda w, n: w.reshape(KD, P, n, P).transpose(2, 1, 0, 3)
    return {
        "x": x[0],
        "positions": positions[0].reshape(NT, P).T,
        "cols": np.concatenate([col[n].reshape(-1, P).T for n in COLS], axis=1),
        "rows": np.broadcast_to(np.concatenate([row[n] for n in ROWS])[None], (P, N_ROWS)),
        "causal": causal.reshape(NT, P, T).transpose(1, 0, 2),
        "bias_a": bias_a.reshape(NT, P, T, H_A).transpose(1, 3, 0, 2),
        "bias_b": bias_b.reshape(NT, P, T, H_B).transpose(1, 3, 0, 2),
        "mla_w_down": mla_w_down[0], "mla_w_uq": mla_w_uq[0], "mla_w_ukv": mla_w_ukv[0], "mla_w_o": mla_w_o[0],
        "gla_w_in": gla_w_in[0], "gla_w_g2": gla_w_g2[0], "gla_w_o": gla_w_o[0],
        "w_query0": peer_w_query[0], "w_query1": peer_w_query[1],
        "sub_keys": peer_sub_keys.transpose(0, 3, 1, 2),
        "peer_u": peer_u.reshape(2, NK, NK, KD, P).transpose(0, 1, 4, 3, 2),
        "peer_v": peer_v.reshape(2, NK, NK, D),
        "w_in_2": w_in_2[0], "w_branch_a": w_branch_a_2[0], "w_branch_b": w_branch_b_2[0], "w_out": w_out_2[0],
        "w_gate_up": np.stack([tiles(w_gate_2[0], NFT), tiles(w_up_2[0], NFT)], axis=2),
        "w_down_2": w_down_2[0].reshape(NFT, P, D),
    }


def kernel(**inputs):
    import concourse.bacc as bacc
    from concourse.bass_utils import run_bass_kernel_spmd

    arrays = {n: np.ascontiguousarray(a) for n, a in layout(**{n: np.asarray(a) for n, a in inputs.items()}).items()}
    nc = bacc.Bacc("TRN2", target_bir_lowering=False, num_devices=1, dynamic_dma_scratch_size=1024)
    dram = {n: nc.dram_tensor(f"in_{n}", a.shape, mybir.dt.from_np(a.dtype), kind="ExternalInput").ap()
            for n, a in arrays.items()}
    out = nc.dram_tensor("out_h", (1, T, D), F32, kind="ExternalOutput").ap()
    build_program(nc, dram, out)
    r = run_bass_kernel_spmd(nc, [{f"in_{n}": a for n, a in arrays.items()}], core_ids=[0])
    return r.results[0]["out_h"]
```

```python
import math
from contextlib import ExitStack

import numpy as np

import concourse.bass as bass
from concourse import mybir

ALU = mybir.AluOpType
ACT = mybir.ActivationFunctionType
AX_X = mybir.AxisListType.X
F32 = mybir.dt.float32
F32R = mybir.dt.float32r
I32 = mybir.dt.int32
U32 = mybir.dt.uint32

P = 128
D = 1024
KD = D // P
T = 256
NT = T // P
EPS = 1e-6

H_MLA, NOPE, ROPE, DV = 16, 64, 32, 64
QK = NOPE + ROPE
HALF = ROPE // 2
R_Q, R_KV = 384, 256
W_DOWN = R_Q + R_KV + ROPE

H_G, DK_G, DV_G, R_G, TAU, CH = 4, 128, 256, 16, 16.0, 64
NCH = T // CH
G_Q, G_K, G_V, G_R, G_LOW = 0, 512, 1024, 2048, 3072
W_GLA = G_LOW + R_G

H_P, NK, TOPK = 8, 128, 16
SLOTS = H_P * TOPK

DH, H_A, H_B, KV_B = 64, 8, 8, 2
A_W = H_A * DH
A_Q, A_K, A_V, B_Q, B_K, B_V, GATE_A, GATE_B = 0, 512, 1024, 1536, 2048, 2176, 2304, 3328
W_IN2 = 4352
FFN = 2816
NFT = FFN // P

NEG = -1e30

COLS = {}
_at = 0
for _name, _n in (("attn0", KD), ("attn1", KD), ("ffn0", KD), ("ffn1", KD), ("mix2", KD), ("ffn2", KD),
                  ("q_lat", R_Q // P), ("kv_lat", R_KV // P), ("b_g", H_G), ("one", KD), ("eps", 1)):
    COLS[_name] = (_at, _n)
    _at += _n
N_COLS = _at

ROWS = {}
_at = 0
for _name, _n in (("qn", QK), ("kn", QK), ("on", DV_G), ("qa", DH), ("ka", DH), ("qb", DH), ("kb", DH),
                  ("sink", H_B), ("freq", HALF)):
    ROWS[_name] = (_at, _n)
    _at += _n
N_ROWS = _at


class Signal:

    def __init__(self, sem):
        self.sem, self.base = sem, 0

    def at(self, n):
        return n + self.base

    def advance(self, n):
        self.base += n


class Chain:

    def __init__(self, sem):
        self.sem, self.count = sem, 0

    def link(self, eng, ins):
        self.count += 1
        ins.then_inc(self.sem, 1)
        eng.wait_ge(self.sem, self.count)


class Kernel:
    def __init__(self, nc, ctx, dram):
        self.nc, self.ctx, self.dram = nc, ctx, dram
        self.signals, self.named = {}, {}
        self.bank = [ctx.enter_context(nc.psum_tensor(f"bank{i}", [P, 512], F32)) for i in range(8)]
        self.act_chain = Chain(ctx.enter_context(nc.semaphore("act_chain")))
        self.dve_chain = Chain(ctx.enter_context(nc.semaphore("dve_chain")))
        self.pool_chain = Chain(ctx.enter_context(nc.semaphore("pool_chain")))
        self.ident = self.sb(ctx, "ident", [P, P])
        self.cols = self.sb(ctx, "cols", [P, N_COLS])
        self.rows = self.sb(ctx, "rows", [P, N_ROWS])
        self.h = self.sb(ctx, "h", [P, NT, D])
        self.xh = self.sb(ctx, "xh", [P, KD, T], F32R)
        self.xl = self.sb(ctx, "xl", [P, KD, T], F32R)

    def sb(self, ctx, name, shape, dt=F32):
        self.named[name] = self.named.get(name, 0) + 1
        return ctx.enter_context(self.nc.sbuf_tensor(f"{name}_{self.named[name]}", shape, dt))

    def sig(self, name):
        if name not in self.signals:
            self.signals[name] = Signal(self.ctx.enter_context(self.nc.semaphore(name)))
        return self.signals[name]

    def col(self, name):
        a, n = COLS[name]
        return self.cols[:, a:a + n]

    def row(self, name):
        a, n = ROWS[name]
        return self.rows[:, a:a + n]


def setup(k):
    loaded, built = k.sig("setup_loaded"), k.sig("setup_built")
    with k.nc.Block() as block:

        @block.sync
        def _(sp):
            sp.dma_start(k.h[:], k.dram["x"].rearrange("(a p) d -> p a d", p=P)).then_inc(loaded.sem, 16)
            sp.dma_start(k.cols[:], k.dram["cols"]).then_inc(loaded.sem, 16)
            sp.dma_start(k.rows[:], k.dram["rows"]).then_inc(loaded.sem, 16)
            sp.wait_ge(loaded.sem, 48)

        @block.gpsimd
        def _(pool):
            pool.memset(k.ident[:], 0.0).then_inc(built.sem, 1)
            pool.wait_ge(built.sem, 1)
            pool.affine_select(out=k.ident[:], in_=k.ident[:], compare_op=ALU.not_equal, fill=1.0, base=0,
                               pattern=[[-1, P]], channel_multiplier=1).then_inc(built.sem, 1)
            pool.wait_ge(built.sem, 2)


def transposes(k, jobs):
    turned, act_out, dve_out = k.sig("tr_turned"), k.sig("tr_act_out"), k.sig("tr_dve_out")
    nb = 4
    acts = [sum(j[1] is not None for j in jobs[:n]) for n in range(len(jobs) + 1)]
    dves = [sum(j[2] is not None for j in jobs[:n]) for n in range(len(jobs) + 1)]
    with k.nc.Block() as block:

        @block.scalar
        def _(act):
            for n, (_, act_copy, _) in enumerate(jobs):
                if act_copy:
                    act.wait_ge(turned.sem, turned.at(n + 1))
                    act_copy(act, k.bank[n % nb]).then_inc(act_out.sem, 1)

        @block.vector
        def _(dve):
            for n, (_, act_copy, dve_copy) in enumerate(jobs):
                if dve_copy:
                    dve.wait_ge(turned.sem, turned.at(n + 1))
                    if act_copy:
                        dve.wait_ge(act_out.sem, act_out.at(acts[n + 1]))
                    dve_copy(dve, k.bank[n % nb]).then_inc(dve_out.sem, 1)

        @block.tensor
        def _(pe):
            for n, (blocks, _, _) in enumerate(jobs):
                if n >= nb:
                    pe.wait_ge(act_out.sem, act_out.at(acts[n - nb + 1]))
                    pe.wait_ge(dve_out.sem, dve_out.at(dves[n - nb + 1]))
                for src, rows, c0 in blocks:
                    last = pe.transpose(k.bank[n % nb][0:rows, c0:c0 + P], src, k.ident[:])
                last.then_inc(turned.sem, 1)

    turned.advance(len(jobs))
    act_out.advance(acts[-1])
    dve_out.advance(dves[-1])


def split_jobs(k, src, kt, xh, xl, gain):
    jobs = []
    for c in range(kt):
        blocks = [(src[:, a, c * P:(c + 1) * P], P, a * P) for a in range(NT)]

        def act_copy(act, bank, c=c):
            return act.activation(xh[:, c, :], bank[:, 0:T], ACT.Copy, scale=gain[:, c:c + 1])

        def dve_copy(dve, bank, c=c):
            return dve.scalar_tensor_tensor(out=xl[:, c, :], in0=bank[:, 0:T], scalar=gain[:, c:c + 1],
                                            in1=xh[:, c, :].bitcast(F32), op0=ALU.mult, op1=ALU.subtract)

        jobs.append((blocks, act_copy, dve_copy))
    return jobs


def norm_groups(k, groups):
    sq, rs, ln = k.sig("nm_squared"), k.sig("nm_summed"), k.sig("nm_rstd")
    with k.nc.Block() as block:

        @block.scalar
        def _(act):
            for n, (src, _, _, work, _) in enumerate(groups):
                act.activation(work, src, ACT.Square).then_inc(sq.sem, 1)
            for n, (src, _, _, _, sums) in enumerate(groups):
                act.wait_ge(rs.sem, rs.at(n + 1))
                last = act.activation(sums, sums, ACT.Ln, scale=1.0 / src.shape[-1], bias=k.col("eps"))
            k.act_chain.link(act, last)
            for _, _, _, _, sums in groups:
                act.activation(sums, sums, ACT.Exp, scale=-0.5).then_inc(ln.sem, 1)

        @block.vector
        def _(dve):
            for n, (_, _, _, work, sums) in enumerate(groups):
                dve.wait_ge(sq.sem, sq.at(n + 1))
                dve.tensor_reduce(sums, work, AX_X, ALU.add).then_inc(rs.sem, 1)
            for n, (src, out, gain, _, sums) in enumerate(groups):
                dve.wait_ge(ln.sem, ln.at(n + 1))
                shape = list(src.shape)
                last = dve.tensor_tensor(out, src, sums.unsqueeze(2).broadcast_to(shape), ALU.mult)
                if gain is not None:
                    k.dve_chain.link(dve, last)
                    last = dve.tensor_tensor(out, out, gain.unsqueeze(1).broadcast_to(shape), ALU.mult)
            k.dve_chain.link(dve, last)

    for s in (sq, rs, ln):
        s.advance(len(groups))


def norm_split(k, gain):
    rooted = k.sig("ns_rooted")
    with ExitStack() as ctx:
        y = k.sb(ctx, "ns_y", [P, NT, D])
        s = k.sb(ctx, "ns_s", [P, NT])
        with k.nc.Block() as block:

            @block.scalar
            def _(act):
                for a in range(NT):
                    k.act_chain.link(act, act.activation(y[:, a], k.h[:, a], ACT.Square, accum_out=s[:, a:a + 1]))
                k.act_chain.link(act, act.activation(s[:], s[:], ACT.Ln, scale=1.0 / D, bias=k.col("eps")))
                act.activation(s[:], s[:], ACT.Exp, scale=-0.5).then_inc(rooted.sem, 1)
                act.wait_ge(rooted.sem, rooted.at(1))
                k.act_chain.link(act, act.activation(y[:, 1], k.h[:, 1], ACT.Copy, scale=s[:, 1:2]))

            @block.vector
            def _(dve):
                dve.wait_ge(rooted.sem, rooted.at(1))
                k.dve_chain.link(dve, dve.tensor_scalar(y[:, 0], k.h[:, 0], s[:, 0:1], None, ALU.mult))

        rooted.advance(1)
        transposes(k, split_jobs(k, y, KD, k.xh, k.xl, k.col(gain)))


def gemm(k, xh, xl, kt, w, n_out, width, out, add=False):
    blk = 2 if kt % 2 == 0 else kt
    ring = 4
    per = kt // blk
    chunks = n_out // width
    assert chunks * width == n_out and width <= 512 and (chunks <= 4 or per % ring == 0)
    loaded = [k.sig(f"gm_loaded{s}") for s in range(ring)]
    hi, lo, used = k.sig("gm_hi"), k.sig("gm_lo"), k.sig("gm_used")
    act_freed, dve_freed = k.sig("gm_act_freed"), k.sig("gm_dve_freed")
    pairs = (chunks - 1) // 2 if chunks > 4 else 0
    with ExitStack() as ctx:
        raw = k.sb(ctx, "gm_raw", [P, ring, blk, width])
        wh = k.sb(ctx, "gm_wh", [P, 2, width], F32R)
        wl = k.sb(ctx, "gm_wl", [P, 2, width], F32R)

        def chunked(eng, body, after=None):
            body(0, 0)
            if pairs:
                with eng.Fori(0, pairs) as m:
                    body(2 * m + 1, 1)
                    body(2 * m + 2, 2)
            for c in range(1 + 2 * pairs, chunks):
                body(c, c)
            if after:
                after()

        with k.nc.Block() as block:

            @block.sync
            def _(sp):
                def body(c, like):
                    for b in range(per):
                        n, slot = c * per + b, (like * per + b) % ring
                        if not (isinstance(n, int) and n < ring):
                            sp.wait_ge(lo.sem, lo.at((n - ring + 1) * blk))
                        sp.dma_start(raw[:, slot, :, :],
                                     w[b * blk * P:(b + 1) * blk * P, bass.ds(c * width, width)]
                                     .rearrange("(k p) n -> p k n", p=P)).then_inc(loaded[slot].sem, 16)
                chunked(sp, body)

            def arrived(eng, c, like, b):
                n, slot = c * per + b, (like * per + b) % ring
                eng.wait_ge(loaded[slot].sem, loaded[slot].at((n - slot) * (16 // ring) + 16))

            @block.scalar
            def _(act):
                def evacuate(c, like):
                    if not add:
                        act.wait_ge(used.sem, used.at((c + 1) * kt))
                        act.activation(out[:, 0, bass.ds(c * width, width)], k.bank[2 * (like % 2)][:, 0:width],
                                       ACT.Copy).then_inc(act_freed.sem, 1)

                def body(c, like):
                    for u in range(kt):
                        if u % blk == 0:
                            arrived(act, c, like, u // blk)
                        n, slot = c * kt + u, (like * kt + u) % 2
                        if not (isinstance(n, int) and n < 2):
                            act.wait_ge(used.sem, used.at(n - 1))
                        act.activation(wh[:, slot, :], raw[:, (like * per + u // blk) % ring, u % blk, :],
                                       ACT.Copy).then_inc(hi.sem, 1)
                        if u == 1 and not (isinstance(c, int) and c == 0):
                            evacuate(c - 1, like - 1)
                chunked(act, body, lambda: evacuate(chunks - 1, chunks - 1))

            @block.vector
            def _(dve):
                def evacuate(c, like):
                    dve.wait_ge(used.sem, used.at((c + 1) * kt))
                    if add:
                        for a in range(NT):
                            o = out[:, a, bass.ds(c * width, width)]
                            dve.tensor_tensor(o, o, k.bank[2 * (like % 2) + a][:, 0:width], ALU.add)\
                               .then_inc(dve_freed.sem, 1)
                    else:
                        dve.tensor_copy(out[:, 1, bass.ds(c * width, width)],
                                        k.bank[2 * (like % 2) + 1][:, 0:width]).then_inc(dve_freed.sem, 1)

                def body(c, like):
                    for u in range(kt):
                        n, slot = c * kt + u, (like * kt + u) % 2
                        dve.wait_ge(hi.sem, hi.at(n + 1))
                        dve.tensor_tensor(wl[:, slot, :], raw[:, (like * per + u // blk) % ring, u % blk, :],
                                          wh[:, slot, :].bitcast(F32), ALU.subtract).then_inc(lo.sem, 1)
                        if u == 1 and not (isinstance(c, int) and c == 0):
                            evacuate(c - 1, like - 1)
                chunked(dve, body, lambda: evacuate(chunks - 1, chunks - 1))

            @block.tensor
            def _(pe):
                def body(c, like):
                    if not (isinstance(c, int) and c < 2):
                        pe.wait_ge(dve_freed.sem, dve_freed.at((c - 1) * (2 if add else 1)))
                        if not add:
                            pe.wait_ge(act_freed.sem, act_freed.at(c - 1))
                    for u in range(kt):
                        n, slot = c * kt + u, (like * kt + u) % 2
                        pe.wait_ge(hi.sem, hi.at(n + 1))
                        ps = [k.bank[2 * (like % 2) + a][:, 0:width] for a in range(NT)]
                        for x in (xh, xl):
                            for a in range(NT):
                                pe.matmul(ps[a], x[:, u, a * P:(a + 1) * P], wh[:, slot, :],
                                          start=(u == 0 and x is xh), stop=False)
                        pe.wait_ge(lo.sem, lo.at(n + 1))
                        for a in range(NT):
                            last = pe.matmul(ps[a], xh[:, u, a * P:(a + 1) * P], wl[:, slot, :],
                                             start=False, stop=(u == kt - 1))
                        last.then_inc(used.sem, 1)
                chunked(pe, body)

    for s in (hi, lo, used):
        s.advance(chunks * kt)
    dve_freed.advance(chunks * (2 if add else 1))
    act_freed.advance(0 if add else chunks)
    blocks = chunks * per
    for slot, x in enumerate(loaded):
        x.advance(16 * ((blocks - slot + ring - 1) // ring))


def narrow_gemm(k, w, c0, width, out):
    loaded, done = k.sig("nw_loaded"), k.sig("nw_done")
    with ExitStack() as ctx:
        raw = k.sb(ctx, "nw_raw", [P, KD, width])
        x = k.sb(ctx, "nw_x", [P, KD, T])
        with k.nc.Block() as block:

            @block.sync
            def _(sp):
                with k.nc.allow_non_contiguous_dma(reason="a few columns"):
                    sp.dma_start(raw[:], w[:, c0:c0 + width].rearrange("(k p) n -> p k n", p=P))\
                      .then_inc(loaded.sem, 16)

            @block.vector
            def _(dve):
                dve.tensor_tensor(x[:], k.xh[:].bitcast(F32), k.xl[:].bitcast(F32), ALU.add).then_inc(done.sem, 1)
                dve.wait_ge(done.sem, done.at(2))
                for a in range(NT):
                    k.dve_chain.link(dve, dve.tensor_copy(out[:, a, c0:c0 + width], k.bank[a][:, 0:width]))

            @block.tensor
            def _(pe):
                pe.wait_ge(loaded.sem, loaded.at(16))
                pe.wait_ge(done.sem, done.at(1))
                for u in range(KD):
                    for a in range(NT):
                        last = pe.matmul(k.bank[a][:, 0:width], x[:, u, a * P:(a + 1) * P], raw[:, u, :],
                                         start=(u == 0), stop=(u == KD - 1))
                last.then_inc(done.sem, 1)

    loaded.advance(16)
    done.advance(2)


def attention(k, heads, q_of, k_of, v_of, bias_of, scale, oh, ol, sink=None):
    scored, masked, powered, scaled = k.sig("at_scored"), k.sig("at_masked"), k.sig("at_powered"), k.sig("at_scaled")
    turned, copied, valued = k.sig("at_turned"), k.sig("at_copied"), k.sig("at_valued")
    high, low = k.sig("at_high"), k.sig("at_low")
    R = 3
    S, PT, O = k.bank[0:3], k.bank[3:5], k.bank[5:7]
    with ExitStack() as ctx:
        s_sb = k.sb(ctx, "at_s", [P, R, NT, T])
        p_sb = k.sb(ctx, "at_p", [P, R, NT, T])
        pt_sb = k.sb(ctx, "at_pt", [P, 2, NT, T])
        peak = k.sb(ctx, "at_peak", [P, R, NT])
        npeak = k.sb(ctx, "at_npeak", [P, R, NT])
        total = k.sb(ctx, "at_total", [P, R, NT])
        esink = k.sb(ctx, "at_esink", [P, R, NT])
        inv = k.sb(ctx, "at_inv", [P, R, NT])
        pairs = heads // 2
        with k.nc.Block() as block:

            @block.tensor
            def _(pe):
                def scores(h):
                    if h >= R:
                        pe.wait_ge(masked.sem, masked.at(h - R + 1))
                    for a in range(NT):
                        last = pe.matmul(S[h % R][:, a * T:(a + 1) * T], q_of(h)[:, a * P:(a + 1) * P], k_of(h),
                                         start=True, stop=True)
                    last.then_inc(scored.sem, 1)

                def apply(h):
                    pe.wait_ge(copied.sem, copied.at(h + 1))
                    if h % 2 == 0 and h >= 4:
                        pe.wait_ge(low.sem, low.at(h // 2 - 1))
                    o = O[h // 2 % 2][DV * (h % 2):DV * (h % 2) + DV, 0:T]
                    for b in range(NT):
                        last = pe.matmul(o, v_of(h, b), pt_sb[:, h % 2, b, :], start=(b == 0), stop=(b == NT - 1))
                    last.then_inc(valued.sem, 1)

                scores(0)
                scores(1)
                for h in range(heads):
                    if h + 2 < heads:
                        scores(h + 2)
                    pe.wait_ge(scaled.sem, scaled.at(h + 1))
                    if h >= 2:
                        pe.wait_ge(copied.sem, copied.at(h - 1))
                    for b in range(NT):
                        for a in range(NT):
                            last = pe.transpose(PT[h % 2][:, b * T + a * P:b * T + (a + 1) * P],
                                                p_sb[:, h % R, a, b * P:(b + 1) * P], k.ident[:])
                    last.then_inc(turned.sem, 1)
                    if h >= 1:
                        apply(h - 1)
                apply(heads - 1)

            @block.vector
            def _(dve):
                def link(ins):
                    k.dve_chain.link(dve, ins)

                def mask(h):
                    r = h % R
                    s = s_sb[:, r]
                    dve.wait_ge(scored.sem, scored.at(h + 1))
                    if h >= R:
                        dve.wait_ge(powered.sem, powered.at(h - R + 1))
                    link(dve.scalar_tensor_tensor(out=s, in0=S[r][:].rearrange("p (a t) -> p a t", a=NT), scalar=scale,
                                                  in1=bias_of(h), op0=ALU.mult, op1=ALU.add))
                    link(dve.tensor_reduce(peak[:, r], s, AX_X, ALU.max))
                    if sink is not None:
                        link(dve.tensor_scalar(peak[:, r], peak[:, r], sink[:, h:h + 1], None, ALU.max))
                        link(dve.tensor_scalar(esink[:, r], peak[:, r], -1.0, sink[:, h:h + 1], ALU.mult, ALU.add))
                    dve.tensor_scalar(npeak[:, r], peak[:, r], -1.0, None, ALU.mult).then_inc(masked.sem, 1)

                def normalise(h):
                    r = h % R
                    dve.wait_ge(powered.sem, powered.at(h + 1))
                    if sink is not None:
                        link(dve.tensor_tensor(total[:, r], total[:, r], esink[:, r], ALU.add))
                    link(dve.reciprocal(inv[:, r], total[:, r]))
                    for a in range(NT):
                        last = dve.tensor_scalar(p_sb[:, r, a], p_sb[:, r, a], inv[:, r, a:a + 1], None, ALU.mult)
                    last.then_inc(scaled.sem, 1)

                def low_part(c):
                    dve.wait_ge(high.sem, high.at(c + 1))
                    dve.tensor_tensor(ol[:, c, :], O[c % 2][:, 0:T], oh[:, c, :].bitcast(F32), ALU.subtract)\
                       .then_inc(low.sem, 1)

                mask(0)
                mask(1)
                for h in range(heads):
                    normalise(h)
                    if h + 2 < heads:
                        mask(h + 2)
                    if h % 2 == 1 and h >= 3:
                        low_part(h // 2 - 1)
                low_part(pairs - 1)

            @block.scalar
            def _(act):
                def power(h):
                    r = h % R
                    act.wait_ge(masked.sem, masked.at(h + 1))
                    if h >= R:
                        act.wait_ge(turned.sem, turned.at(h - R + 1))
                    if sink is not None:
                        act.activation(esink[:, r], esink[:, r], ACT.Exp)
                    for a in range(NT):
                        last = act.activation(p_sb[:, r, a], s_sb[:, r, a], ACT.Exp, bias=npeak[:, r, a:a + 1],
                                              accum_out=total[:, r, a:a + 1])
                    last.then_inc(powered.sem, 1)

                def high_part(c):
                    act.wait_ge(valued.sem, valued.at(2 * c + 2))
                    act.activation(oh[:, c, :], O[c % 2][:, 0:T], ACT.Copy).then_inc(high.sem, 1)

                power(0)
                power(1)
                for h in range(heads):
                    act.wait_ge(turned.sem, turned.at(h + 1))
                    if h >= 2:
                        act.wait_ge(valued.sem, valued.at(h - 1))
                    act.activation(pt_sb[:, h % 2].rearrange("p a t -> p (a t)"), PT[h % 2][:], ACT.Copy)\
                       .then_inc(copied.sem, 1)
                    if h + 2 < heads:
                        power(h + 2)
                    if h % 2 == 1 and h >= 3:
                        high_part(h // 2 - 1)
                high_part(pairs - 1)

    for s in (scored, masked, powered, scaled, turned, copied, valued):
        s.advance(heads)
    for s in (high, low):
        s.advance(pairs)


def angles(k, cs):
    loaded, reduced, done = k.sig("ro_loaded"), k.sig("ro_reduced"), k.sig("ro_done")
    c1 = 6.28125
    c2 = float(np.float32(np.round((2 * math.pi - c1) * 2 ** 22) / 2 ** 22))
    c3 = 2 * math.pi - c1 - c2
    magic = 1.5 * 2 ** 23
    with ExitStack() as ctx:
        pos = k.sb(ctx, "ro_pos", [P, NT], I32)
        posf = k.sb(ctx, "ro_posf", [P, NT])
        ang = k.sb(ctx, "ro_ang", [P, NT, HALF])
        turns = k.sb(ctx, "ro_turns", [P, NT, 2, HALF])
        with k.nc.Block() as block:

            @block.sync
            def _(sp):
                sp.dma_start(pos[:], k.dram["positions"]).then_inc(loaded.sem, 16)

            @block.vector
            def _(dve):
                def link(ins):
                    k.dve_chain.link(dve, ins)
                dve.wait_ge(loaded.sem, 16)
                link(dve.tensor_copy(posf[:], pos[:]))
                for a in range(NT):
                    link(dve.tensor_scalar(ang[:, a], k.row("freq"), posf[:, a:a + 1], None, ALU.mult))
                for s in range(2):
                    t = turns[:, :, s]
                    link(dve.tensor_scalar(t, ang[:], 1.0 / (2 * math.pi), 0.25 * s, ALU.mult, ALU.add))
                    link(dve.tensor_scalar(t, t, magic, None, ALU.add))
                    link(dve.tensor_scalar(t, t, magic, None, ALU.subtract))
                    r = cs[:, :, s]
                    link(dve.scalar_tensor_tensor(out=r, in0=t, scalar=-c1, in1=ang[:], op0=ALU.mult, op1=ALU.add))
                    link(dve.scalar_tensor_tensor(out=r, in0=t, scalar=-c2, in1=r, op0=ALU.mult, op1=ALU.add))
                    link(dve.scalar_tensor_tensor(out=r, in0=t, scalar=-c3, in1=r, op0=ALU.mult, op1=ALU.add))
                    if s:
                        link(dve.tensor_scalar(r, r, math.pi / 2, None, ALU.add))
                    link(dve.tensor_scalar(r, r, 3.1415925, -3.1415925, ALU.min, ALU.max))
                dve.sem_inc(reduced.sem, 1)

            @block.scalar
            def _(act):
                act.wait_ge(reduced.sem, 1)
                act.activation(cs[:], cs[:], ACT.Sin).then_inc(done.sem, 1)
                act.wait_ge(done.sem, 1)


def mla(k):
    norm_split(k, "attn0")
    with ExitStack() as ctx:
        cs = k.sb(ctx, "ml_cs", [P, NT, 2, HALF])
        angles(k, cs)
        v = k.sb(ctx, "ml_v", [P, NT, H_MLA, NOPE + DV])
        qt = k.sb(ctx, "ml_qt", [QK, H_MLA, T])
        kt = k.sb(ctx, "ml_kt", [QK, H_MLA, T])
        with ExitStack() as inner:
            down = k.sb(inner, "ml_down", [P, NT, W_DOWN])
            q = k.sb(inner, "ml_q", [P, NT, H_MLA, QK])
            kk = k.sb(inner, "ml_k", [P, NT, H_MLA, QK])
            gemm(k, k.xh, k.xl, KD, k.dram["mla_w_down"], W_DOWN, W_DOWN // 2, down)
            with ExitStack() as lat:
                y = k.sb(lat, "ml_y", [P, NT, R_Q + R_KV])
                s = k.sb(lat, "ml_s", [P, 2, NT])
                c_q, c_kv = slice(0, R_Q), slice(R_Q, R_Q + R_KV)
                norm_groups(k, [(down[:, :, c], y[:, :, c], None, y[:, :, c], s[:, n])
                                for n, c in enumerate((c_q, c_kv))])
                transposes(k, split_jobs(k, y[:, :, c_q], R_Q // P, k.xh, k.xl, k.col("q_lat"))
                           + split_jobs(k, y[:, :, c_kv], R_KV // P, k.xh[:, 4:], k.xl[:, 4:], k.col("kv_lat")))
            gemm(k, k.xh, k.xl, R_Q // P, k.dram["mla_w_uq"], H_MLA * QK, 512,
                 q[:].rearrange("p a h d -> p a (h d)"))
            gemm(k, k.xh[:, 4:], k.xl[:, 4:], R_KV // P, k.dram["mla_w_ukv"], H_MLA * (NOPE + DV), 512,
                 v[:].rearrange("p a h d -> p a (h d)"))
            head_norm_rope(k, down, v, q, kk, cs)
            jobs = []
            for dst, src in ((qt, q), (kt, kk)):
                for h in range(0, H_MLA, 2):
                    blocks = [(src[:, a, h + i], QK, i * T + a * P) for i in range(2) for a in range(NT)]
                    o = dst[:, h:h + 2].rearrange("p h t -> p (h t)")
                    if h % 4:
                        jobs.append((blocks, None, lambda dve, b, o=o: dve.tensor_copy(o, b[0:QK, :])))
                    else:
                        jobs.append((blocks, lambda act, b, o=o: act.activation(o, b[0:QK, :], ACT.Copy), None))
            transposes(k, jobs)
        causal = k.sb(ctx, "ml_causal", [P, NT, T])
        load(k, causal[:], k.dram["causal"])
        attention(k, H_MLA, lambda h: qt[:, h], lambda h: kt[:, h], lambda h, b: v[:, b, h, NOPE:], lambda h: causal[:],
                  QK ** -0.5, k.xh, k.xl)
    gemm(k, k.xh, k.xl, KD, k.dram["mla_w_o"], D, 512, k.h, add=True)


def load(k, dst, src):
    loaded = k.sig("ld_loaded")
    with k.nc.Block() as block:

        @block.sync
        def _(sp):
            sp.dma_start(dst, src).then_inc(loaded.sem, 16)
            sp.wait_ge(loaded.sem, loaded.at(16))

    loaded.advance(16)


def head_norm_rope(k, down, kv, q, kk, cs):
    copied = k.sig("hr_copied")
    with k.nc.Block() as block:

        @block.vector
        def _(dve):
            k.dve_chain.link(dve, dve.tensor_copy(kk[:, :, :, 0:NOPE].rearrange("p a h d -> p (a h) d"),
                                                  kv[:, :, :, 0:NOPE].rearrange("p a h d -> p (a h) d")))

        @block.scalar
        def _(act):
            for a in range(NT):
                k.act_chain.link(act, act.activation(
                    kk[:, a, :, NOPE:QK],
                    down[:, a, R_Q + R_KV:W_DOWN].unsqueeze(1).broadcast_to([P, H_MLA, ROPE]), ACT.Copy))

    with ExitStack() as ctx:
        work = k.sb(ctx, "hr_work", [P, NT * H_MLA, QK])
        work2 = k.sb(ctx, "hr_work2", [P, NT * H_MLA, QK])
        s = k.sb(ctx, "hr_s", [P, 2, NT * H_MLA])
        flat = [x[:].rearrange("p a h d -> p (a h) d") for x in (q, kk)]
        norm_groups(k, [(x, x, k.row(gain), w[:], s[:, n])
                        for n, (x, gain, w) in enumerate(zip(flat, ("qn", "kn"), (work, work2)))])
        t = k.sb(ctx, "hr_t", [P, 2, 4, H_MLA, HALF])

        def rope(eng, chain, x, t):
            for a in range(NT):
                x1, x2 = x[:, a, :, NOPE:NOPE + HALF], x[:, a, :, NOPE + HALF:QK]
                sin, cos = (cs[:, a, s].unsqueeze(1).broadcast_to([P, H_MLA, HALF]) for s in range(2))
                for n, (f, g) in enumerate(((x1, cos), (x2, sin), (x2, cos), (x1, sin))):
                    last = eng.tensor_tensor(t[:, n], f, g, ALU.mult)
                chain.link(eng, last)
                eng.tensor_tensor(x1, t[:, 0], t[:, 1], ALU.subtract)
                chain.link(eng, eng.tensor_tensor(x2, t[:, 2], t[:, 3], ALU.add))

        with k.nc.Block() as block:

            @block.vector
            def _(dve):
                rope(dve, k.dve_chain, q, t[:, 0])

            @block.gpsimd
            def _(pool):
                rope(pool, k.pool_chain, kk, t[:, 1])




def key_scores(k, l, s):
    with ExitStack() as inner:
        q = k.sb(inner, "pk_q", [P, NT, D])
        qt = k.sb(inner, "pk_qt", [P, H_P, T])
        keys = k.sb(inner, "pk_keys", [P, 2, NK])
        gemm(k, k.xh, k.xl, KD, k.dram[f"w_query{l}"], D, 512, q)
        jobs = []
        for h in range(0, H_P, 2):
            blocks = [(q[:, a, (h + i) * P:(h + i + 1) * P], P, i * T + a * P) for i in range(2) for a in range(NT)]
            o = qt[:, h:h + 2].rearrange("p h t -> p (h t)")
            jobs.append((blocks, None, lambda dve, b, o=o: dve.tensor_copy(o, b[:])) if h % 4 else
                        (blocks, lambda act, b, o=o: act.activation(o, b[:], ACT.Copy), None))
        transposes(k, jobs)
        zeroed, loaded, scored = k.sig("pk_zeroed"), k.sig("pk_loaded"), k.sig("pk_scored")
        with k.nc.Block() as block:

            @block.gpsimd
            def _(pool):
                pool.memset(keys[:], 0.0).then_inc(zeroed.sem, 1)

            @block.sync
            def _(sp):
                sp.wait_ge(zeroed.sem, zeroed.at(1))
                for c in range(2):
                    sp.dma_start(keys[c * 64:(c + 1) * 64, c, :], k.dram["sub_keys"][l, :, c, :])\
                      .then_inc(loaded.sem, 16)

            @block.tensor
            def _(pe):
                pe.wait_ge(loaded.sem, loaded.at(32))
                for h in range(H_P):
                    for a in range(NT):
                        last = pe.matmul(k.bank[h][:, a * T:(a + 1) * T], qt[:, h, a * P:(a + 1) * P],
                                         keys[:].rearrange("p c n -> p (c n)"), start=True, stop=True)
                    last.then_inc(scored.sem, 1)

            def banks(eng, copy, first, chain):
                for h in range(first, H_P, 2):
                    eng.wait_ge(scored.sem, scored.at(h + 1))
                    chain.link(eng, copy(s[:, :, h].rearrange("p a c n -> p a (c n)"),
                                         k.bank[h][:].rearrange("p (a n) -> p a n", a=NT)))

            @block.scalar
            def _(act):
                banks(act, lambda o, i: act.activation(o, i, ACT.Copy), 0, k.act_chain)

            @block.vector
            def _(dve):
                banks(dve, dve.tensor_copy, 1, k.dve_chain)

        zeroed.advance(1)
        loaded.advance(32)
        scored.advance(H_P)


RAW = 4


def rank_and_first(k, l, s, expert, gate, hidden):
    G = NT * H_P
    names = ("a_hi", "a_lo", "first", "bent")
    a_hi, a_lo, first, bent = (k.sig(f"rf_{x}") for x in names)
    landed = [k.sig(f"rf_landed{r}") for r in range(RAW)]
    with ExitStack() as ctx:
        top = k.sb(ctx, "pk_top", [P, G, 2, TOPK])
        at = k.sb(ctx, "pk_at", [P, G, 2, TOPK], U32)
        atf = k.sb(ctx, "pk_atf", [P, G, 2, TOPK])
        cand = s[:].rearrange("p a h c (x y) -> p (a h) (c x) y", y=TOPK)
        best = k.sb(ctx, "pk_best", [P, G, TOPK])
        pos = k.sb(ctx, "pk_pos", [P, G, TOPK], U32)
        half = k.sb(ctx, "pk_half", [P, 2, G, TOPK], U32)
        halff = k.sb(ctx, "pk_halff", [P, 2, G, TOPK])
        hot = cand
        total = k.sb(ctx, "pk_total", [P, G])
        count = k.sb(ctx, "pk_count", [P, TOPK], I32)
        countf = k.sb(ctx, "pk_countf", [P, TOPK])
        counted, raised, powered = k.sig("pk_counted"), k.sig("pk_raised"), k.sig("pk_powered")
        raw = k.sb(ctx, "rf_raw", [P, RAW, KD, P])
        ah = k.sb(ctx, "rf_ah", [P, 2, KD, P], F32R)
        al = k.sb(ctx, "rf_al", [P, 2, KD, P], F32R)

        def looped(eng, step):
            for r in range(RAW):
                step(r, r, True)
            with eng.Fori(1, NK // RAW - 1) as m:
                for r in range(RAW):
                    step(RAW * m + r, r, True)
            for r in range(RAW):
                step(NK - RAW + r, r, r < RAW - 1)

        def past(i, least):
            return not isinstance(i, int) or i >= least

        def flat(x, r):
            return x[:, r].rearrange("p k e -> p (k e)")

        with k.nc.Block() as block:

            @block.sync
            def _(sp):
                def step(i, r, more):
                    if past(i, RAW):
                        sp.wait_ge(a_lo.sem, a_lo.at(i - RAW + 1))
                    sp.dma_start(flat(raw, r),
                                 k.dram["peer_u"][l, bass.ds(i, 1)].rearrange("o p k e -> p (o k e)"))\
                      .then_inc(landed[r].sem, 16)
                looped(sp, step)

            @block.tensor
            def _(pe):
                def step(i, raw_slot, more):
                    r = raw_slot % 2
                    if past(i, 2):
                        pe.wait_ge(bent.sem, bent.at(i - 1))
                    ps = k.bank[r][:, 0:T]
                    pe.wait_ge(a_hi.sem, a_hi.at(i + 1))
                    for c in range(KD):
                        pe.matmul(ps, ah[:, r, c], k.xh[:, c], start=(c == 0), stop=False)
                        pe.matmul(ps, ah[:, r, c], k.xl[:, c], start=False, stop=False)
                    pe.wait_ge(a_lo.sem, a_lo.at(i + 1))
                    for c in range(KD):
                        last = pe.matmul(ps, al[:, r, c], k.xh[:, c], start=False, stop=(c == KD - 1))
                    last.then_inc(first.sem, 1)
                looped(pe, step)

            @block.gpsimd
            def _(pool):
                pool.iota(count[:], [[1, TOPK]], base=0, channel_multiplier=0).then_inc(counted.sem, 1)

                def step(i, r, more):
                    pool.wait_ge(a_hi.sem, a_hi.at(i + 1))
                    pool.tensor_tensor(flat(al, r % 2), flat(raw, r), flat(ah, r % 2).bitcast(F32), ALU.subtract)\
                        .then_inc(a_lo.sem, 1)
                looped(pool, step)

            @block.vector
            def _(dve):
                def ordered(steps):
                    for ins in steps:
                        last = ins
                    k.dve_chain.link(dve, last)

                def top16(rows):
                    ordered(dve.max(m[:, 0:8], v) for v, m, _ in rows)
                    ordered(dve.max_index(i[:, 0:8], m[:, 0:8], v) for v, m, i in rows)
                    ordered(dve.match_replace(v, m[:, 0:8], v, -3.0e38) for v, m, _ in rows)
                    ordered(dve.max(m[:, 8:16], v) for v, m, _ in rows)
                    ordered(dve.max_index(i[:, 8:16], m[:, 8:16], v) for v, m, i in rows)

                top16([(s[:, g // H_P, g % H_P, c], top[:, g, c], at[:, g, c]) for g in range(G) for c in range(2)])
                dve.wait_ge(counted.sem, counted.at(1))
                ordered([dve.tensor_copy(countf[:], count[:]), dve.tensor_copy(atf[:], at[:]),
                         dve.tensor_tensor(cand, top[:, :, 0].unsqueeze(3).broadcast_to([P, G, TOPK, TOPK]),
                                           top[:, :, 1].unsqueeze(2).broadcast_to([P, G, TOPK, TOPK]), ALU.add)])
                top16([(cand[:, g].rearrange("p a b -> p (a b)"), best[:, g], pos[:, g]) for g in range(G)])
                ordered([dve.tensor_scalar(half[:, 0], pos[:], 4, None, ALU.logical_shift_right),
                         dve.tensor_scalar(half[:, 1], pos[:], 15, None, ALU.bitwise_and)])
                dve.tensor_tensor(gate[:], best[:], best[:, :, 0:1].broadcast_to([P, G, TOPK]), ALU.subtract)\
                   .then_inc(raised.sem, 1)
                ordered([dve.tensor_copy(halff[:], half[:])])
                for c in range(2):
                    wide = [P, G, TOPK, TOPK]
                    ordered([dve.tensor_tensor(hot, halff[:, c].unsqueeze(3).broadcast_to(wide),
                                               countf[:].unsqueeze(1).unsqueeze(1).broadcast_to(wide), ALU.is_equal)])
                    ordered([dve.tensor_tensor(hot, hot, atf[:, :, c].unsqueeze(2).broadcast_to(wide),
                                               ALU.mult)])
                    ordered([dve.tensor_reduce(expert[:, c], hot, AX_X, ALU.add)])
                dve.wait_ge(powered.sem, powered.at(1))
                ordered([dve.tensor_reduce(total[:], gate[:], AX_X, ALU.add)])
                ordered([dve.reciprocal(total[:], total[:])])
                ordered([dve.tensor_tensor(gate[:], gate[:], total[:].unsqueeze(2).broadcast_to([P, G, TOPK]),
                                           ALU.mult)])

            @block.scalar
            def _(act):
                def high(i, r):
                    act.wait_ge(landed[r].sem, landed[r].at((i - r) * (16 // RAW) + 16))
                    if past(i, 2):
                        act.wait_ge(first.sem, first.at(i - 1))
                    act.activation(flat(ah, r % 2), flat(raw, r), ACT.Copy).then_inc(a_hi.sem, 1)

                def step(i, r, more):
                    if more:
                        high(i + 1, (r + 1) % RAW)
                    act.wait_ge(first.sem, first.at(i + 1))
                    act.activation(hidden[:, bass.ds(i, 1), :].rearrange("p o t -> p (o t)"), k.bank[r % 2][:, 0:T],
                                   ACT.Gelu).then_inc(bent.sem, 1)

                high(0, 0)
                looped(act, step)
                act.wait_ge(raised.sem, raised.at(1))
                act.activation(gate[:], gate[:], ACT.Exp).then_inc(powered.sem, 1)

        for x in (counted, raised, powered):
            x.advance(1)
        for x in (a_hi, a_lo, first, bent):
            x.advance(NK)
        for x in landed:
            x.advance(16 // RAW * NK)


def turn_slots(k, expert, gate, slots):
    jobs = []
    for n, src in enumerate((expert[:, 0], expert[:, 1], gate[:])):
        flat = src.rearrange("p g s -> p (g s)")
        jobs.append(([(flat[:, a * SLOTS:(a + 1) * SLOTS], P, a * P) for a in range(NT)], None,
                     lambda dve, b, o=slots[:, n]: dve.tensor_copy(o, b[:, 0:T])))
    transposes(k, jobs)


def apply_gates(k, slots, hidden):
    names = ("hot_j", "equal", "hot_i", "summed", "even_applied", "odd_copied", "odd_applied")
    hot_j, equal, hot_i, summed, even_applied, odd_copied, odd_applied = (k.sig(f"ag_{x}") for x in names)
    counted = k.sig("ag_counted")
    N, R = 4, 4
    groups = T // N
    with ExitStack() as ctx:
        count = k.sb(ctx, "ag_count", [P, NK], I32)
        countf = k.sb(ctx, "ag_countf", [P, NK])
        a = k.sb(ctx, "ag_a", [P, R, N, NK])
        b = k.sb(ctx, "ag_b", [P, R, N, NK])
        odd = k.sb(ctx, "ag_odd", [P, 2, NK, N])

        def looped(eng, body):
            for r in range(R):
                body(r, r)
            with eng.Fori(1, groups // R) as m:
                for r in range(R):
                    body(R * m + r, r)

        def again(n):
            return not isinstance(n, int)

        def places(n, x):
            return slots[:, x, bass.ds(n * N, N)].unsqueeze(2).broadcast_to([P, N, NK])

        with k.nc.Block() as block:

            @block.gpsimd
            def _(pool):
                k.pool_chain.link(pool, pool.iota(count[:], [[1, NK]], base=0, channel_multiplier=0))
                pool.tensor_copy(countf[:], count[:]).then_inc(counted.sem, 1)

                def body(n, r):
                    pool.wait_ge(equal.sem, equal.at(n + 1))
                    pool.tensor_tensor(b[:, r], b[:, r], places(n, 2), ALU.mult).then_inc(hot_i.sem, 1)

                def apply(n, r):
                    pool.wait_ge(odd_copied.sem, odd_copied.at((n + 1) // 2))
                    h = hidden[:, :, bass.ds(n * N, N)]
                    pool.tensor_tensor(h, h, odd[:, r // 2], ALU.mult).then_inc(odd_applied.sem, 1)

                for n in range(R):
                    body(n, n)
                    if n == 3:
                        apply(n - 2, n - 2)
                with pool.Fori(1, groups // R) as m:
                    for r in range(R):
                        body(R * m + r, r)
                        if r % 2:
                            apply(R * m + r - 2, (r - 2) % R)
                apply(groups - 1, R - 1)

            @block.scalar
            def _(act):
                def copy(n, r, again):
                    act.wait_ge(summed.sem, summed.at(n + 1))
                    if again:
                        act.wait_ge(odd_applied.sem, odd_applied.at((n - 3) // 2))
                    act.activation(odd[:, r // 2], k.bank[r][:].rearrange("p (t i) -> p i t", t=N), ACT.Copy)\
                       .then_inc(odd_copied.sem, 1)

                for r in (1, 3):
                    copy(r, r, False)
                with act.Fori(1, groups // R) as m:
                    for r in (1, 3):
                        copy(R * m + r, r, True)

            @block.vector
            def _(dve):
                dve.wait_ge(counted.sem, counted.at(1))
                numbers = countf[:].unsqueeze(1).broadcast_to([P, N, NK])

                def one_hots(n, r):
                    if again(n):
                        dve.wait_ge(summed.sem, summed.at(n - R + 1))
                    dve.tensor_tensor(b[:, r], numbers, places(n, 0), ALU.is_equal).then_inc(equal.sem, 1)
                    dve.tensor_tensor(a[:, r], numbers, places(n, 1), ALU.is_equal).then_inc(hot_j.sem, 1)

                def apply(n, r):
                    dve.wait_ge(summed.sem, summed.at(n + 1))
                    h = hidden[:, :, bass.ds(n * N, N)]
                    dve.tensor_tensor(h, h, k.bank[r][:].rearrange("p (t i) -> p i t", t=N), ALU.mult)\
                       .then_inc(even_applied.sem, 1)

                LEAD = 2
                for n in range(R):
                    one_hots(n, n)
                    if n == LEAD:
                        apply(n - LEAD, n - LEAD)
                with dve.Fori(1, groups // R) as m:
                    for r in range(R):
                        one_hots(R * m + r, r)
                        if r % 2 == 0:
                            apply(R * m + r - LEAD, (r - LEAD) % R)
                apply(groups - LEAD, R - LEAD)

            @block.tensor
            def _(pe):
                def body(n, r):
                    pe.wait_ge(hot_j.sem, hot_j.at(n + 1))
                    pe.wait_ge(hot_i.sem, hot_i.at(n + 1))
                    if again(n) and r % 2:
                        pe.wait_ge(odd_copied.sem, odd_copied.at((n - R + 1) // 2))
                    elif again(n):
                        pe.wait_ge(even_applied.sem, even_applied.at((n - R) // 2 + 1))
                    for t in range(N):
                        last = pe.matmul(k.bank[r][:, t * NK:(t + 1) * NK], a[:, r, t], b[:, r, t],
                                         start=True, stop=True)
                    last.then_inc(summed.sem, 1)
                looped(pe, body)

    counted.advance(1)
    for x in (hot_j, equal, hot_i, summed):
        x.advance(groups)
    for x in (even_applied, odd_copied, odd_applied):
        x.advance(groups // 2)


def second_products(k, l, hidden):
    names = ("b_hi", "b_lo", "m_hi", "m_lo", "second")
    b_hi, b_lo, m_hi, m_lo, second = (k.sig(f"sp_{x}") for x in names)
    landed = [k.sig(f"sp_landed{r}") for r in range(RAW)]
    W = D // 2
    with ExitStack() as ctx:
        raw = k.sb(ctx, "sp_raw", [P, RAW, D])
        bh = k.sb(ctx, "sp_bh", [P, 2, D], F32R)
        bl = k.sb(ctx, "sp_bl", [P, 2, D], F32R)
        mh = k.sb(ctx, "sp_mh", [P, 2, T], F32R)
        ml = k.sb(ctx, "sp_ml", [P, 2, T], F32R)

        def looped(eng, step):
            for r in range(RAW):
                step(r, r)
            with eng.Fori(1, NK // RAW - 1) as m:
                for r in range(RAW):
                    step(RAW * m + r, r)
            for r in range(RAW):
                step(NK - RAW + r, r)

        def past(i, least):
            return not isinstance(i, int) or i >= least

        def row(i):
            return hidden[:, bass.ds(i, 1), :].rearrange("p o t -> p (o t)")

        def bank(a, c):
            return k.bank[2 * a + c][:]

        with k.nc.Block() as block:

            @block.sync
            def _(sp):
                def step(i, r):
                    if past(i, RAW):
                        sp.wait_ge(b_lo.sem, b_lo.at(2 * (i - RAW + 1)))
                    sp.dma_start(raw[:, r], k.dram["peer_v"][l, bass.ds(i, 1)].rearrange("o p d -> p (o d)"))\
                      .then_inc(landed[r].sem, 16)
                looped(sp, step)

            @block.scalar
            def _(act):
                def step(i, r):
                    act.wait_ge(landed[r].sem, landed[r].at((i - r) * (16 // RAW) + 16))
                    src, r = raw[:, r], r % 2
                    for c in range(2):
                        if past(i, 2):
                            act.wait_ge(second.sem, second.at(2 * i + c - 3))
                        half = slice(c * W, (c + 1) * W)
                        act.activation(bh[:, r, half], src[:, half], ACT.Copy).then_inc(b_hi.sem, 1)
                        if c == 0:
                            if past(i, 2):
                                act.wait_ge(second.sem, second.at(2 * (i - 1)))
                            act.activation(mh[:, r], row(i), ACT.Copy).then_inc(m_hi.sem, 1)
                looped(act, step)

            @block.vector
            def _(dve):
                def step(i, r):
                    src, r = raw[:, r], r % 2
                    for c in range(2):
                        half = slice(c * W, (c + 1) * W)
                        dve.wait_ge(b_hi.sem, b_hi.at(2 * i + c + 1))
                        dve.tensor_tensor(bl[:, r, half], src[:, half], bh[:, r, half].bitcast(F32), ALU.subtract)\
                           .then_inc(b_lo.sem, 1)
                        if c == 0:
                            dve.wait_ge(m_hi.sem, m_hi.at(i + 1))
                            dve.tensor_tensor(ml[:, r], row(i), mh[:, r].bitcast(F32), ALU.subtract)\
                               .then_inc(m_lo.sem, 1)
                looped(dve, step)
                dve.wait_ge(second.sem, second.at(2 * NK))
                for a in range(NT):
                    for c in range(2):
                        o = k.h[:, a, c * W:(c + 1) * W]
                        k.dve_chain.link(dve, dve.tensor_tensor(o, o, bank(a, c), ALU.add))

            @block.tensor
            def _(pe):
                def step(i, raw_slot):
                    r = raw_slot % 2
                    first = isinstance(i, int) and i == 0
                    final = isinstance(i, int) and i == NK - 1
                    pe.wait_ge(m_lo.sem, m_lo.at(i + 1))
                    for c in range(2):
                        pe.wait_ge(b_lo.sem, b_lo.at(2 * i + c + 1))
                        half = slice(c * W, (c + 1) * W)
                        for a in range(NT):
                            t = slice(a * P, (a + 1) * P)
                            for x, (m, b) in enumerate(((mh, bh), (mh, bl), (ml, bh))):
                                last = pe.matmul(bank(a, c), m[:, r, t], b[:, r, half], start=(first and x == 0),
                                                 stop=(final and x == 2), skip_group_check=True)
                        last.then_inc(second.sem, 1)
                looped(pe, step)

    for x in (b_hi, b_lo, second):
        x.advance(2 * NK)
    for x in (m_hi, m_lo):
        x.advance(NK)
    for x in landed:
        x.advance(16 // RAW * NK)


def two_products(k, name, n, na, a_dram, b_dram, gates=None):
    s = {x: k.sig(f"{name}_{x}") for x in ("a_hi", "a_lo", "b_hi", "b_lo", "first", "bent", "middle", "m_hi",
                                           "m_lo", "second")}
    a_in = [k.sig(f"{name}_a_in{r}") for r in range(2)]
    b_in = [k.sig(f"{name}_b_in{r}") for r in range(2)]
    with ExitStack() as ctx:
        a_raw = k.sb(ctx, f"{name}_a_raw", [P, 2, na, D])
        b_raw = k.sb(ctx, f"{name}_b_raw", [P, 2, D])
        ah = k.sb(ctx, f"{name}_ah", [P, 2, na, KD, P], F32R)
        al = k.sb(ctx, f"{name}_al", [P, 2, na, KD, P], F32R)
        bh = k.sb(ctx, f"{name}_bh", [P, 2, D], F32R)
        bl = k.sb(ctx, f"{name}_bl", [P, 2, D], F32R)
        bent = k.sb(ctx, f"{name}_bent", [P, 2, T])
        mid = k.sb(ctx, f"{name}_mid", [P, 2, T])
        mh = k.sb(ctx, f"{name}_mh", [P, 2, T], F32R)
        ml = k.sb(ctx, f"{name}_ml", [P, 2, T], F32R)

        def first_ps(r, x):
            return k.bank[r][:, x * T:(x + 1) * T]

        def second_ps(a, c):
            return k.bank[4 + 2 * a + c][:]

        def stepped(eng, step):
            def fixed(i):
                step(i, i % 2, i < n, i >= 2, i + 1 < n)
            for i in range(4):
                fixed(i)
            if n > 8:
                with eng.Fori(0, (n - 6) // 2) as m:
                    step(2 * m + 4, 0, True, True, True)
                    step(2 * m + 5, 1, True, True, True)
            for i in range(n - 2 if n > 8 else 4, n + 2):
                fixed(i)

        def past(i, least):
            return not (isinstance(i, int) and i < least)

        with k.nc.Block() as block:

            @block.sync
            def _(sp):
                def load_a(i, r):
                    if past(i, 2):
                        sp.wait_ge(s["a_lo"].sem, s["a_lo"].at(i - 1))
                    sp.dma_start(a_raw[:, r], a_dram(i)).then_inc(a_in[r].sem, 16)

                def step(i, r, first, second, ahead):
                    if ahead:
                        load_a(i + 1, 1 - r)
                    if past(i, 1) and (not isinstance(i, int) or i <= n):
                        if past(i, 3):
                            sp.wait_ge(s["b_lo"].sem, s["b_lo"].at(i - 2))
                        sp.dma_start(b_raw[:, 1 - r], b_dram(i - 1)).then_inc(b_in[1 - r].sem, 16)

                load_a(0, 0)
                stepped(sp, step)

            def landed(eng, sems, i, r):
                eng.wait_ge(sems[r].sem, sems[r].at((i - r) * 8 + 16))

            @block.scalar
            def _(act):
                def split_a(i, r):
                    landed(act, a_in, i, r)
                    if past(i, 2):
                        act.wait_ge(s["first"].sem, s["first"].at(i - 1))
                    act.activation(ah[:, r].rearrange("p x k e -> p (x k e)"),
                                   a_raw[:, r].rearrange("p x n -> p (x n)"), ACT.Copy).then_inc(s["a_hi"].sem, 1)

                def step(i, r, first, second, ahead):
                    if ahead:
                        split_a(i + 1, 1 - r)
                    if first:
                        act.wait_ge(s["first"].sem, s["first"].at(i + 1))
                        if past(i, 2):
                            act.wait_ge(s["middle"].sem, s["middle"].at(i - 1))
                        if na == 1:
                            act.activation(bent[:, r], first_ps(r, 0), ACT.Gelu).then_inc(s["bent"].sem, 1)
                        else:
                            act.activation(bent[:, r], first_ps(r, 0), ACT.Silu).then_inc(s["bent"].sem, 1)
                    if past(i, 1) and (not isinstance(i, int) or i <= n):
                        landed(act, b_in, i - 1, 1 - r)
                        if past(i, 3):
                            act.wait_ge(s["second"].sem, s["second"].at(i - 2))
                        act.activation(bh[:, 1 - r], b_raw[:, 1 - r], ACT.Copy).then_inc(s["b_hi"].sem, 1)
                    if first:
                        act.wait_ge(s["middle"].sem, s["middle"].at(i + 1))
                        if past(i, 2):
                            act.wait_ge(s["second"].sem, s["second"].at(i - 1))
                        act.activation(mh[:, r], mid[:, r], ACT.Copy).then_inc(s["m_hi"].sem, 1)

                split_a(0, 0)
                stepped(act, step)

            @block.vector
            def _(dve):
                links = k.dve_chain

                def split_a(i, r):
                    dve.wait_ge(s["a_hi"].sem, s["a_hi"].at(i + 1))
                    dve.tensor_tensor(al[:, r].rearrange("p x k e -> p (x k e)"),
                                      a_raw[:, r].rearrange("p x n -> p (x n)"),
                                      ah[:, r].bitcast(F32).rearrange("p x k e -> p (x k e)"), ALU.subtract)\
                       .then_inc(s["a_lo"].sem, 1)

                def step(i, r, first, second, ahead):
                    if ahead:
                        split_a(i + 1, 1 - r)
                    if first:
                        dve.wait_ge(s["bent"].sem, s["bent"].at(i + 1))
                        if past(i, 2):
                            dve.wait_ge(s["m_lo"].sem, s["m_lo"].at(i - 1))
                        if na == 1:
                            dve.tensor_tensor(mid[:, r], bent[:, r], gates[:, i, :], ALU.mult)\
                               .then_inc(s["middle"].sem, 1)
                        else:
                            dve.tensor_tensor(mid[:, r], bent[:, r], first_ps(r, 1), ALU.mult)\
                               .then_inc(s["middle"].sem, 1)
                    if past(i, 1) and (not isinstance(i, int) or i <= n):
                        dve.wait_ge(s["b_hi"].sem, s["b_hi"].at(i))
                        dve.tensor_tensor(bl[:, 1 - r], b_raw[:, 1 - r], bh[:, 1 - r].bitcast(F32), ALU.subtract)\
                           .then_inc(s["b_lo"].sem, 1)
                    if first:
                        dve.wait_ge(s["m_hi"].sem, s["m_hi"].at(i + 1))
                        dve.tensor_tensor(ml[:, r], mid[:, r], mh[:, r].bitcast(F32), ALU.subtract)\
                           .then_inc(s["m_lo"].sem, 1)

                split_a(0, 0)
                stepped(dve, step)
                dve.wait_ge(s["second"].sem, s["second"].at(n))
                for a in range(NT):
                    for c in range(2):
                        o = k.h[:, a, c * 512:(c + 1) * 512]
                        links.link(dve, dve.tensor_tensor(o, o, second_ps(a, c), ALU.add))

            @block.tensor
            def _(pe):
                def step(i, r, first, second, ahead):
                    if first:
                        pe.wait_ge(s["a_hi"].sem, s["a_hi"].at(i + 1))
                        pe.wait_ge(s["a_lo"].sem, s["a_lo"].at(i + 1))
                        if past(i, 2):
                            pe.wait_ge(s["middle"].sem, s["middle"].at(i - 1))
                        for x in range(na):
                            for c in range(KD):
                                pe.matmul(first_ps(r, x), ah[:, r, x, c], k.xh[:, c], start=(c == 0), stop=False)
                                pe.matmul(first_ps(r, x), ah[:, r, x, c], k.xl[:, c], start=False, stop=False)
                                last = pe.matmul(first_ps(r, x), al[:, r, x, c], k.xh[:, c], start=False,
                                                 stop=(c == KD - 1))
                        last.then_inc(s["first"].sem, 1)
                    if second:
                        for x in ("b_hi", "b_lo", "m_hi", "m_lo"):
                            pe.wait_ge(s[x].sem, s[x].at(i - 1))
                        start = isinstance(i, int) and i == 2
                        stop = isinstance(i, int) and i == n + 1
                        for a in range(NT):
                            t = slice(a * P, (a + 1) * P)
                            for x, (m, b) in enumerate(((mh, bh), (mh, bl), (ml, bh))):
                                for c in range(2):
                                    last = pe.matmul(second_ps(a, c), m[:, r, t], b[:, r, c * 512:(c + 1) * 512],
                                                     start=(start and x == 0), stop=(stop and x == 2),
                                                     skip_group_check=True)
                        last.then_inc(s["second"].sem, 1)
                stepped(pe, step)

    for x in s.values():
        x.advance(n)
    for r in range(2):
        a_in[r].advance(8 * n)
        b_in[r].advance(8 * n)


def peer(k, l):
    norm_split(k, f"ffn{l}")
    with ExitStack() as ctx:
        expert = k.sb(ctx, "pe_expert", [P, 2, NT * H_P, TOPK])
        gate = k.sb(ctx, "pe_gate", [P, NT * H_P, TOPK])
        hidden = k.sb(ctx, "pe_hidden", [P, NK, T])
        with ExitStack() as inner:
            s = k.sb(inner, "pe_s", [P, NT, H_P, 2, NK])
            key_scores(k, l, s)
            rank_and_first(k, l, s, expert, gate, hidden)
        with ExitStack() as inner:
            slots = k.sb(inner, "pe_slots", [P, 3, T])
            turn_slots(k, expert, gate, slots)
            apply_gates(k, slots, hidden)
        second_products(k, l, hidden)


def gla(k):
    norm_split(k, "attn1")
    with ExitStack() as ctx:
        proj = k.sb(ctx, "gl_proj", [P, NT, W_GLA])
        gemm(k, k.xh, k.xl, KD, k.dram["gla_w_in"], G_LOW, 512, proj)
        narrow_gemm(k, k.dram["gla_w_in"], G_LOW, R_G, proj)
        o = k.sb(ctx, "gl_o", [P, NT, H_G, DV_G])
        with ExitStack() as inner:
            gla_core(k, inner, proj, o)
        gated_output(k, proj, o)
        transposes(k, split_jobs(k, o[:].rearrange("p a h d -> p a (h d)"), KD, k.xh, k.xl, k.col("one")))
    gemm(k, k.xh, k.xl, KD, k.dram["gla_w_o"], D, 512, k.h, add=True)


def gla_core(k, ctx, proj, o):
    N = H_G * NT
    qt = k.sb(ctx, "gl_qt", [P, H_G, T])
    kt = k.sb(ctx, "gl_kt", [P, H_G, T])
    low = k.sb(ctx, "gl_low", [R_G, T])
    jobs = []
    for dst, c0 in ((qt, G_Q), (kt, G_K)):
        for h in range(0, H_G, 2):
            blocks = [(proj[:, a, c0 + (h + i) * DK_G:c0 + (h + i + 1) * DK_G], P, i * T + a * P)
                      for i in range(2) for a in range(NT)]
            d = dst[:, h:h + 2].rearrange("p h t -> p (h t)")
            jobs.append((blocks, None, lambda dve, b, d=d: dve.tensor_copy(d, b[:])) if h % 4 else
                        (blocks, lambda act, b, d=d: act.activation(d, b[:], ACT.Copy), None))
    jobs.append(([(proj[:, a, G_LOW:W_GLA], R_G, a * P) for a in range(NT)], None,
                 lambda dve, b: dve.tensor_copy(low[:], b[0:R_G, 0:T])))
    transposes(k, jobs)

    w2 = k.sb(ctx, "gl_w2", [R_G, H_G * DK_G])
    z = k.sb(ctx, "gl_z", [P, H_G, T])
    e = k.sb(ctx, "gl_e", [P, H_G, T])
    fresh = k.sb(ctx, "gl_fresh", [P, H_G, NCH, CH])
    b = k.sb(ctx, "gl_b", [P, H_G, NCH, CH])
    left = k.sb(ctx, "gl_left", [P, H_G, NCH, CH])
    qd = k.sb(ctx, "gl_qd", [P, H_G, T])
    ki = k.sb(ctx, "gl_ki", [P, H_G, T])
    kd = k.sb(ctx, "gl_kd", [P, H_G, T])
    decay = k.sb(ctx, "gl_decay", [P, H_G, NCH])
    load(k, w2[:], k.dram["gla_w_g2"])
    made, folded, logged, summed, powered = (k.sig(f"gl_{x}") for x in ("made", "folded", "logged", "summed",
                                                                       "powered"))
    masked = k.sig("gl_masked")
    with k.nc.Block() as block:

        @block.tensor
        def _(pe):
            for h in range(H_G):
                pe.matmul(k.bank[h][:, 0:T], w2[:, h * DK_G:(h + 1) * DK_G], low[:], start=True, stop=True)\
                  .then_inc(made.sem, 1)

        @block.gpsimd
        def _(pool):
            k.pool_chain.link(pool, pool.memset(fresh[:], 1.0))
            k.pool_chain.link(pool, pool.memset(fresh[:, :, :, 0:1], 0.0))
            pool.nop().then_inc(masked.sem, 1)

        @block.vector
        def _(dve):
            def link(ins):
                k.dve_chain.link(dve, ins)
            dve.wait_ge(made.sem, made.at(H_G))
            for h in range(H_G):
                ins = dve.tensor_scalar(z[:, h], k.bank[h][:, 0:T], k.col("b_g")[:, h:h + 1], None, ALU.add)
            link(ins)
            dve.scalar_tensor_tensor(out=e[:], in0=z[:], scalar=-1.0, in1=z[:], op0=ALU.mult, op1=ALU.min)\
               .then_inc(folded.sem, 1)
            link(dve.tensor_scalar(z[:], z[:], 0.0, None, ALU.min))
            dve.wait_ge(logged.sem, logged.at(1))
            link(dve.tensor_tensor(z[:], z[:], e[:], ALU.subtract))
            link(dve.tensor_scalar(z[:], z[:], 1.0 / TAU, None, ALU.mult))
            dve.wait_ge(masked.sem, masked.at(1))
            link(dve.tensor_tensor_scan(b[:].rearrange("p h n c -> p (h n c)"),
                                        fresh[:].rearrange("p h n c -> p (h n c)"),
                                        z[:].rearrange("p h t -> p (h t)"), 0.0, ALU.mult, ALU.add))
            dve.tensor_tensor(left[:], b[:, :, :, CH - 1:CH].broadcast_to([P, H_G, NCH, CH]), b[:], ALU.subtract)\
               .then_inc(summed.sem, 1)
            flat = [x[:].rearrange("p h t -> p (h t)") for x in (qt, kt, qd, ki, kd)]
            dve.wait_ge(powered.sem, powered.at(1))
            dve.scalar_tensor_tensor(out=flat[2], in0=flat[0], scalar=DK_G ** -0.5,
                                     in1=qd[:].rearrange("p h t -> p (h t)"), op0=ALU.mult, op1=ALU.mult)
            dve.wait_ge(powered.sem, powered.at(2))
            dve.tensor_tensor(flat[3], flat[1], flat[3], ALU.mult)
            dve.wait_ge(powered.sem, powered.at(3))
            link(dve.tensor_tensor(flat[4], flat[1], flat[4], ALU.mult))

        @block.scalar
        def _(act):
            act.wait_ge(folded.sem, folded.at(1))
            k.act_chain.link(act, act.activation(e[:], e[:], ACT.Exp))
            act.activation(e[:], e[:], ACT.Ln, bias=k.col("one")[:, 0:1]).then_inc(logged.sem, 1)
            act.wait_ge(summed.sem, summed.at(1))
            act.activation(qd[:], b[:].rearrange("p h n c -> p h (n c)"), ACT.Exp).then_inc(powered.sem, 1)
            act.activation(ki[:], b[:].rearrange("p h n c -> p h (n c)"), ACT.Exp, scale=-1.0).then_inc(powered.sem, 1)
            act.activation(kd[:], left[:].rearrange("p h n c -> p h (n c)"), ACT.Exp).then_inc(powered.sem, 1)
            k.act_chain.link(act, act.activation(decay[:], b[:, :, :, CH - 1], ACT.Exp))

    made.advance(H_G)
    powered.advance(3)
    for s in (folded, logged, summed, masked):
        s.advance(1)

    at = k.sb(ctx, "gl_at", [P, N, CH])
    kdn = k.sb(ctx, "gl_kdn", [P, N, DK_G])
    state = k.sb(ctx, "gl_state", [P, NCH - 1, H_G, DV_G])
    weighed, copied, selected = k.sig("gl_weighed"), k.sig("gl_copied"), k.sig("gl_selected")
    turned, keyed, added, carried = k.sig("gl_turned"), k.sig("gl_keyed"), k.sig("gl_added"), k.sig("gl_carried")
    mixed = k.sig("gl_mixed")

    def rows(n):
        return slice(CH * (n % 2), CH * (n % 2) + CH)

    def values(n, h):
        return proj[rows(n), n // 2, G_V + h * DV_G:G_V + (h + 1) * DV_G]

    with k.nc.Block() as block:

        @block.tensor
        def _(pe):
            for h in range(H_G):
                for n in range(NCH):
                    t = slice(n * CH, (n + 1) * CH)
                    g = h * NT + n // 2
                    last = pe.matmul(k.bank[0][rows(n), g * CH:(g + 1) * CH], ki[:, h, t], qd[:, h, t], start=True,
                                     stop=True, skip_group_check=True)
            last.then_inc(weighed.sem, 1)
            for h in range(H_G):
                for a in range(NT):
                    last = pe.transpose(k.bank[1 + h // 2][:, (h % 2 * NT + a) * P:(h % 2 * NT + a + 1) * P],
                                        kd[:, h, a * P:(a + 1) * P], k.ident[:])
            last.then_inc(turned.sem, 1)
            pe.wait_ge(keyed.sem, keyed.at(1))
            for n in range(NCH - 1):
                if n:
                    pe.wait_ge(carried.sem, carried.at(n))
                for h in range(H_G):
                    last = pe.matmul(k.bank[3 + h // 2][:, h % 2 * DV_G:(h % 2 + 1) * DV_G],
                                     kdn[rows(n), h * NT + n // 2], values(n, h), start=True, stop=True)
                last.then_inc(added.sem, 1)
            pe.wait_ge(selected.sem, selected.at(1))
            pe.wait_ge(carried.sem, carried.at(NCH - 1))
            for h in range(H_G):
                for a in range(NT):
                    g = h * NT + a
                    if g >= 3:
                        pe.wait_ge(mixed.sem, mixed.at(g - 2))
                    for n in (2 * a, 2 * a + 1):
                        ps = k.bank[5 + g % 3][rows(n), 0:DV_G]
                        last = pe.matmul(ps, at[rows(n), g], values(n, h), start=True, stop=(n == 0),
                                         skip_group_check=True)
                        if n:
                            last = pe.matmul(ps, qd[:, h, n * CH:(n + 1) * CH], state[:, n - 1, h], start=False,
                                             stop=True, skip_group_check=True)
                    last.then_inc(weighed.sem, 1)

        @block.scalar
        def _(act):
            act.wait_ge(weighed.sem, weighed.at(1))
            act.activation(at[:].rearrange("p g t -> p (g t)"), k.bank[0][:], ACT.Copy).then_inc(copied.sem, 1)
            act.wait_ge(turned.sem, turned.at(1))
            for i in range(2):
                last = act.activation(kdn[:, i * 4:(i + 1) * 4].rearrange("p g d -> p (g d)"), k.bank[1 + i][:],
                                      ACT.Copy)
            last.then_inc(keyed.sem, 1)
            for h in range(H_G):
                for a in range(NT):
                    g = h * NT + a
                    act.wait_ge(weighed.sem, weighed.at(g + 2))
                    act.activation(o[:, a, h], k.bank[5 + g % 3][:, 0:DV_G], ACT.Copy).then_inc(mixed.sem, 1)

        @block.gpsimd
        def _(pool):
            pool.wait_ge(copied.sem, copied.at(1))
            for r in range(2):
                part = at[r * CH:(r + 1) * CH]
                k.pool_chain.link(pool, pool.affine_select(out=part, in_=part, compare_op=ALU.is_ge, fill=0.0,
                                                           base=0, pattern=[[0, N], [1, CH]],
                                                           channel_multiplier=-1))
            pool.nop().then_inc(selected.sem, 1)

        @block.vector
        def _(dve):
            for n in range(NCH - 1):
                dve.wait_ge(added.sem, added.at(n + 1))
                for h in range(H_G):
                    ps = k.bank[3 + h // 2][:, h % 2 * DV_G:(h % 2 + 1) * DV_G]
                    if n == 0:
                        last = dve.tensor_copy(state[:, 0, h], ps)
                    else:
                        last = dve.scalar_tensor_tensor(out=state[:, n, h], in0=state[:, n - 1, h],
                                                        scalar=decay[:, h, n:n + 1], in1=ps, op0=ALU.mult,
                                                        op1=ALU.add)
                last.then_inc(carried.sem, 1)
                dve.wait_ge(carried.sem, carried.at(n + 1))

    weighed.advance(1 + N)
    mixed.advance(N)
    for s in (copied, selected, turned, keyed):
        s.advance(1)
    added.advance(NCH - 1)
    carried.advance(NCH - 1)


def gated_output(k, proj, o):
    with ExitStack() as ctx:
        e = k.sb(ctx, "go_e", [P, NT, D])
        work = k.sb(ctx, "go_work", [P, NT * H_G, DV_G])
        s = k.sb(ctx, "go_s", [P, NT * H_G])
        flat = o[:].rearrange("p a h d -> p (a h) d")
        norm_groups(k, [(flat, flat, k.row("on"), work[:], s[:])])
        powered = k.sig("go_powered")
        r = proj[:, :, G_R:G_R + D]
        with k.nc.Block() as block:

            @block.scalar
            def _(act):
                act.activation(e[:], r, ACT.Silu).then_inc(powered.sem, 1)

            @block.vector
            def _(dve):
                dve.wait_ge(powered.sem, powered.at(1))
                flat_o = o[:].rearrange("p a h d -> p a (h d)")
                k.dve_chain.link(dve, dve.tensor_tensor(flat_o, flat_o, e[:], ALU.mult))

        powered.advance(1)


def second_block(k):
    norm_split(k, "mix2")
    with ExitStack() as ctx:
        proj = k.sb(ctx, "sb_proj", [P, NT, W_IN2])
        w = k.dram["w_in_2"]
        main = W_IN2 // 512 * 512
        gemm(k, k.xh, k.xl, KD, w[:, 0:main], main, 512, proj)
        gemm(k, k.xh, k.xl, KD, w[:, main:W_IN2], W_IN2 - main, W_IN2 - main, proj[:, :, main:W_IN2])
        ya = k.sb(ctx, "sb_ya", [P, NT, D])
        with ExitStack() as inner:
            yb = k.sb(inner, "sb_yb", [P, NT, D])
            bias = k.sb(inner, "sb_bias", [P, H_A, NT, T])
            qt = k.sb(inner, "sb_qt", [P, H_A // 2, T])
            kt = k.sb(inner, "sb_kt", [P, H_A // 2, T])
            qbt = k.sb(inner, "sb_qbt", [P, H_B // 2, T])
            kbt = k.sb(inner, "sb_kbt", [P, KV_B, T])
            with ExitStack() as norms:
                heads = k.sb(norms, "sb_heads", [P, 4, NT * H_A, DH])
                s = k.sb(norms, "sb_s", [P, 4, NT * H_A])
                kb = k.sb(norms, "sb_kb", [P, NT, 2 * KV_B, DH])
                groups = []
                for n, (c0, gain) in enumerate(((A_Q, "qa"), (A_K, "ka"), (B_Q, "qb"))):
                    for a in range(NT):
                        x = proj[:, a, c0:c0 + A_W].rearrange("p (h d) -> p h d", d=DH)
                        at = slice(a * H_A, (a + 1) * H_A)
                        groups.append((x, x, k.row(gain), heads[:, n, at], s[:, n, at]))
                for a in range(NT):
                    x = proj[:, a, B_K:B_K + KV_B * DH].rearrange("p (h d) -> p h d", d=DH)
                    at = slice(a * KV_B, (a + 1) * KV_B)
                    groups.append((x, kb[:, a, 0:KV_B], k.row("kb"), heads[:, 3, at], s[:, 3, at]))
                norm_groups(k, groups)
                swap(k, kb)
                transposes(k, turn_pairs(qt, proj[:, :, A_Q:A_Q + A_W]) + turn_pairs(kt, proj[:, :, A_K:A_K + A_W])
                           + turn_pairs(qbt, proj[:, :, B_Q:B_Q + A_W])
                           + turn_pairs(kbt, kb[:].rearrange("p a h d -> p a (h d)")))

            def half(h):
                return slice(DH * (h % 2), DH * (h % 2) + DH)

            load(k, bias[:], k.dram["bias_a"])
            attention(k, H_A, lambda h: qt[half(h), h // 2], lambda h: kt[half(h), h // 2],
                      lambda h, b: proj[:, b, A_V + h * DH:A_V + (h + 1) * DH], lambda h: bias[:, h], DH ** -0.5,
                      k.xh, k.xl)
            gemm(k, k.xh, k.xl, A_W // P, k.dram["w_branch_a"], D, 512, ya)
            load(k, bias[:], k.dram["bias_b"])

            def key_head(h):
                return h // (H_B // KV_B)

            attention(k, H_B, lambda h: qbt[half(h), h // 2], lambda h: kbt[half(h), (h % 2) ^ key_head(h)],
                      lambda h, b: proj[:, b, B_V + key_head(h) * DH:B_V + (key_head(h) + 1) * DH],
                      lambda h: bias[:, h], DH ** -0.5, k.xh, k.xl, sink=k.row("sink"))
            gemm(k, k.xh, k.xl, A_W // P, k.dram["w_branch_b"], D, 512, yb)
            mix_gates(k, proj, ya, yb)
        transposes(k, split_jobs(k, ya, KD, k.xh, k.xl, k.col("one")))
    gemm(k, k.xh, k.xl, KD, k.dram["w_out"], D, 512, k.h, add=True)
    norm_split(k, "ffn2")
    up, down = k.dram["w_gate_up"], k.dram["w_down_2"]
    two_products(k, "ff", NFT, 2, lambda t: up[bass.ds(t, 1)].rearrange("o p x k e -> p (o x) (k e)"),
                 lambda t: down[bass.ds(t, 1)].rearrange("o p d -> p (o d)"))


def swap(k, kb):
    with k.nc.Block() as block:

        @block.vector
        def _(dve):
            for h in range(KV_B):
                k.dve_chain.link(dve, dve.tensor_copy(kb[:, :, KV_B + h], kb[:, :, KV_B - 1 - h]))


def turn_pairs(dst, src):
    jobs = []
    for c in range(0, dst.shape[1], 2):
        blocks = [(src[:, a, (c + i) * P:(c + i + 1) * P], P, i * T + a * P) for i in range(2) for a in range(NT)]
        d = dst[:, c:c + 2].rearrange("p c t -> p (c t)")
        jobs.append((blocks, None, lambda dve, b, d=d: dve.tensor_copy(d, b[:])) if c % 4 else
                    (blocks, lambda act, b, d=d: act.activation(d, b[:], ACT.Copy), None))
    return jobs


def mix_gates(k, proj, ya, yb):
    powered = k.sig("mg_powered")
    with ExitStack() as ctx:
        e = k.sb(ctx, "mg_e", [P, 2, NT, D])
        with k.nc.Block() as block:

            @block.scalar
            def _(act):
                for n, c0 in enumerate((GATE_A, GATE_B)):
                    act.activation(e[:, n], proj[:, :, c0:c0 + D], ACT.Sigmoid).then_inc(powered.sem, 1)

            @block.vector
            def _(dve):
                for n, y in enumerate((ya, yb)):
                    dve.wait_ge(powered.sem, powered.at(n + 1))
                    k.dve_chain.link(dve, dve.tensor_tensor(e[:, n], y[:], e[:, n], ALU.mult))
                k.dve_chain.link(dve, dve.tensor_tensor(ya[:], e[:, 0], e[:, 1], ALU.add))

    powered.advance(2)


def build_program(nc, dram, out):
    with ExitStack() as ctx:
        k = Kernel(nc, ctx, dram)
        setup(k)
        mla(k)
        peer(k, 0)
        gla(k)
        peer(k, 1)
        second_block(k)
        stored = k.sig("stored")
        with nc.Block() as block:

            @block.sync
            def _(sp):
                sp.dma_start(out.rearrange("b (a p) d -> p (b a) d", p=P), k.h[:]).then_inc(stored.sem, 16)
                sp.wait_ge(stored.sem, 16)


def t5_bucket(rel):
    half = 16
    max_exact = half // 2
    ret = (rel > 0).astype(np.int32) * half
    n = np.abs(rel)
    large = max_exact + (np.log(np.maximum(n, 1) / max_exact) / np.log(128 / max_exact)
                         * (half - max_exact)).astype(np.int32)
    large = np.minimum(large, half - 1)
    return ret + np.where(n < max_exact, n, large)


def layout(x, positions, attn_norm_g, ffn_norm_g, mla_w_down, mla_g_q_lat, mla_w_uq, mla_g_kv_lat, mla_w_ukv,
           mla_g_qn, mla_g_kn, mla_w_o, gla_w_in, gla_w_g2, gla_b_g, gla_g_on, gla_w_o, peer_w_query, peer_sub_keys,
           peer_u, peer_v, norm_mix_2, w_in_2, q_norm_a_2, k_norm_a_2, rpb_a_2, q_norm_b_2, k_norm_b_2, sink_b_2,
           t5_table_2, w_branch_a_2, w_branch_b_2, w_out_2, norm_ffn_2, w_gate_2, w_up_2, w_down_2):
    col = {
        "attn0": attn_norm_g[0], "attn1": attn_norm_g[1], "ffn0": ffn_norm_g[0], "ffn1": ffn_norm_g[1],
        "mix2": norm_mix_2[0], "ffn2": norm_ffn_2[0], "q_lat": mla_g_q_lat[0], "kv_lat": mla_g_kv_lat[0],
        "b_g": gla_b_g[0], "one": np.ones(D, np.float32), "eps": np.full(P, EPS, np.float32),
    }
    freq = np.float32(10000.0) ** (-np.arange(HALF, dtype=np.float32) / np.float32(HALF))
    row = {"qn": mla_g_qn[0], "kn": mla_g_kn[0], "on": gla_g_on[0], "qa": q_norm_a_2[0], "ka": k_norm_a_2[0],
           "qb": q_norm_b_2[0], "kb": k_norm_b_2[0], "sink": sink_b_2[0], "freq": freq}
    q, key = np.arange(T)[:, None], np.arange(T)[None, :]
    qr, qc, kr, kc = q // 64, q % 64, key // 64, key % 64
    start = np.clip(qc - 8, 0, 48)
    near = (kc >= start) & (kc < start + 16)
    bias_a = np.where(near[:, :, None], rpb_a_2[0][kr - qr + 7, np.clip(kc - qc, -15, 15) + 15], np.float32(NEG))
    rel = key - q
    bias_b = np.where((np.abs(rel) <= 128)[:, :, None], t5_table_2[t5_bucket(rel)], np.float32(NEG))
    causal = np.where(key <= q, np.float32(0), np.float32(NEG))
    tiles = lambda w, n: w.reshape(KD, P, n, P).transpose(2, 1, 0, 3)
    return {
        "x": x[0],
        "positions": positions[0].reshape(NT, P).T,
        "cols": np.concatenate([col[n].reshape(-1, P).T for n in COLS], axis=1),
        "rows": np.broadcast_to(np.concatenate([row[n] for n in ROWS])[None], (P, N_ROWS)),
        "causal": causal.reshape(NT, P, T).transpose(1, 0, 2),
        "bias_a": bias_a.reshape(NT, P, T, H_A).transpose(1, 3, 0, 2),
        "bias_b": bias_b.reshape(NT, P, T, H_B).transpose(1, 3, 0, 2),
        "mla_w_down": mla_w_down[0], "mla_w_uq": mla_w_uq[0], "mla_w_ukv": mla_w_ukv[0], "mla_w_o": mla_w_o[0],
        "gla_w_in": gla_w_in[0], "gla_w_g2": gla_w_g2[0], "gla_w_o": gla_w_o[0],
        "w_query0": peer_w_query[0], "w_query1": peer_w_query[1],
        "sub_keys": peer_sub_keys.transpose(0, 3, 1, 2),
        "peer_u": peer_u.reshape(2, NK, NK, KD, P).transpose(0, 1, 4, 3, 2),
        "peer_v": peer_v.reshape(2, NK, NK, D),
        "w_in_2": w_in_2[0], "w_branch_a": w_branch_a_2[0], "w_branch_b": w_branch_b_2[0], "w_out": w_out_2[0],
        "w_gate_up": np.stack([tiles(w_gate_2[0], NFT), tiles(w_up_2[0], NFT)], axis=2),
        "w_down_2": w_down_2[0].reshape(NFT, P, D),
    }


def kernel(**inputs):
    import concourse.bacc as bacc
    from concourse.bass_utils import run_bass_kernel_spmd

    arrays = {n: np.ascontiguousarray(a) for n, a in layout(**{n: np.asarray(a) for n, a in inputs.items()}).items()}
    nc = bacc.Bacc("TRN2", target_bir_lowering=False, num_devices=1, dynamic_dma_scratch_size=1024)
    dram = {n: nc.dram_tensor(f"in_{n}", a.shape, mybir.dt.from_np(a.dtype), kind="ExternalInput").ap()
            for n, a in arrays.items()}
    out = nc.dram_tensor("out_h", (1, T, D), F32, kind="ExternalOutput").ap()
    build_program(nc, dram, out)
    r = run_bass_kernel_spmd(nc, [{f"in_{n}": a for n, a in arrays.items()}], core_ids=[0])
    return r.results[0]["out_h"]
```
